# Optimizing a Trainium2 kernel written in Bass

```python
import jax, jax.numpy as jnp
from jax import lax
import numpy as np

D_MODEL = 2048
BATCH = 1
SEQ = 512
DEPTH = 1
DEC_BATCH = 8
DEC_SEQ = 4
PAST_LEN = 256
PAGE_SIZE = 128

N_META = 16
HEAD_DIM = 128
GDN_HEADS = 8
FOX_HEADS = 8
GDN_WIDTH = GDN_HEADS * HEAD_DIM
FOX_WIDTH = FOX_HEADS * HEAD_DIM
MIX_WIDTH = GDN_WIDTH + FOX_WIDTH
CONV_W = 4
GDN_CONV_DIM = 3 * GDN_WIDTH
GDN_CHUNK = 64
FOX_BLOCK = 128
PEER_HEADS = 8
PEER_KEYS = 128
PEER_EXPERTS = PEER_KEYS * PEER_KEYS
PEER_DKEY = 256
PEER_HALF = PEER_DKEY // 2
PEER_TOPK = 16
PEER_BLOCK = 128
EPS = 1e-6
IN_SIZES = (GDN_CONV_DIM, GDN_HEADS, GDN_HEADS, GDN_WIDTH, 3 * FOX_WIDTH, FOX_HEADS, FOX_WIDTH)
IN_COLS = GDN_CONV_DIM + 2 * GDN_HEADS + GDN_WIDTH + 3 * FOX_WIDTH + FOX_HEADS + FOX_WIDTH

kernel_name = 'hybrid_gdn_fox_peer_step'

def rmsnorm(x, g):
    xf = x.astype(jnp.float32)
    y = xf * lax.rsqrt(jnp.mean(xf * xf, axis=-1, keepdims=True) + EPS)
    return (y * g.astype(jnp.float32)).astype(x.dtype)

def l2norm(x):
    xf = x.astype(jnp.float32)
    return xf * lax.rsqrt(jnp.sum(xf * xf, axis=-1, keepdims=True) + EPS)

def split_in(p):
    return jnp.split(p, [int(s) for s in np.cumsum(IN_SIZES)[:-1]], axis=-1)

def gdn_inputs(conv_in, a, b, conv_w, a_log, dt_bias):
    B, Lp, _ = conv_in.shape
    L = Lp - (CONV_W - 1)
    y = conv_w[0] * conv_in[:, 0:L]
    for i in range(1, CONV_W):
        y = y + conv_w[i] * conv_in[:, i:i + L]
    y = jax.nn.silu(y).reshape(B, L, 3, GDN_HEADS, HEAD_DIM)
    q = jnp.transpose(l2norm(y[:, :, 0]) * (HEAD_DIM ** -0.5), (0, 2, 1, 3))
    k = jnp.transpose(l2norm(y[:, :, 1]), (0, 2, 1, 3))
    v = jnp.transpose(y[:, :, 2].astype(jnp.float32), (0, 2, 1, 3))
    g = -jnp.exp(a_log.astype(jnp.float32)) * jax.nn.softplus(a.astype(jnp.float32) + dt_bias.astype(jnp.float32))
    beta = jax.nn.sigmoid(b.astype(jnp.float32))
    return q, k, v, jnp.transpose(g, (0, 2, 1)), jnp.transpose(beta, (0, 2, 1))

def gdn_chunk(S, q, k, v, g, beta):
    L = q.shape[2]
    G = jnp.cumsum(g, axis=-1)
    causal = jnp.tril(jnp.ones((L, L), dtype=bool))
    decay = jnp.exp(jnp.where(causal, G[..., :, None] - G[..., None, :], -jnp.inf))
    kk = jnp.einsum('bhtk,bhsk->bhts', k, k)
    qk = jnp.einsum('bhtk,bhsk->bhts', q, k)
    a_strict = jnp.tril(beta[..., :, None] * decay * kk, -1)
    eG = jnp.exp(G)
    rhs = beta[..., None] * (v - eG[..., None] * jnp.einsum('bhtk,bhkv->bhtv', k, S))
    u = lax.linalg.triangular_solve(a_strict, rhs, left_side=True, lower=True, unit_diagonal=True)
    o = eG[..., None] * jnp.einsum('bhtk,bhkv->bhtv', q, S) + jnp.einsum('bhts,bhsv->bhtv', qk * decay, u)
    tail = jnp.exp(G[..., -1:] - G)
    S_new = eG[..., -1, None, None] * S + jnp.einsum('bhsk,bhsv->bhkv', k * tail[..., None], u)
    return S_new, o

def to_chunks(t):
    n = t.shape[2] // GDN_CHUNK
    return jnp.moveaxis(t.reshape(t.shape[:2] + (n, GDN_CHUNK) + t.shape[3:]), 2, 0)

def from_chunks(o):
    o = jnp.moveaxis(o, 0, 2)
    return o.reshape(o.shape[:2] + (o.shape[2] * o.shape[3],) + o.shape[4:])

def fox_inputs(qkv, f, f_bias, qnorm, knorm):
    B, L, _ = qkv.shape
    t = qkv.reshape(B, L, 3, FOX_HEADS, HEAD_DIM)
    q = rmsnorm(t[:, :, 0], qnorm)
    k = rmsnorm(t[:, :, 1], knorm)
    v = t[:, :, 2]
    logf = jax.nn.log_sigmoid(f.astype(jnp.float32) + f_bias.astype(jnp.float32))
    return q, k, v, logf

def fox_attend(q, cq, qpos, k, v, ck, kpos):
    s = jnp.einsum('bqhd,bkhd->bhqk', q, k, preferred_element_type=jnp.float32) * (HEAD_DIM ** -0.5)
    s = s + jnp.transpose(cq, (0, 2, 1))[..., :, None] - jnp.transpose(ck, (0, 2, 1))[..., None, :]
    s = jnp.where(kpos[None, :] <= qpos[:, None], s, -jnp.inf)
    p = jax.nn.softmax(s, axis=-1)
    return jnp.einsum('bhqk,bkhd->bqhd', p.astype(v.dtype), v)

def fox_prompt(q, c, k, v):
    B, T = q.shape[:2]
    nb = -(-T // FOX_BLOCK)
    pad = nb * FOX_BLOCK - T
    qb = jnp.moveaxis(jnp.pad(q, ((0, 0), (0, pad), (0, 0), (0, 0))).reshape(B, nb, FOX_BLOCK, FOX_HEADS, HEAD_DIM), 1, 0)
    cb = jnp.moveaxis(jnp.pad(c, ((0, 0), (0, pad), (0, 0))).reshape(B, nb, FOX_BLOCK, FOX_HEADS), 1, 0)
    starts = jnp.arange(nb, dtype=jnp.int32) * FOX_BLOCK
    kpos = jnp.arange(T, dtype=jnp.int32)

    def block(args):
        qi, ci, s0 = args
        return fox_attend(qi, ci, s0 + jnp.arange(FOX_BLOCK, dtype=jnp.int32), k, v, c, kpos)

    o = lax.map(block, (qb, cb, starts))
    return jnp.moveaxis(o, 0, 1).reshape(B, nb * FOX_BLOCK, FOX_HEADS, HEAD_DIM)[:, :T]

def merge_heads(gdn_o, z, fox_o, og, gdn_onorm, fox_onorm, w_out):
    B, L, _ = z.shape
    go = rmsnorm(jnp.transpose(gdn_o, (0, 2, 1, 3)), gdn_onorm).reshape(B, L, GDN_WIDTH) * jax.nn.silu(z)
    fo = rmsnorm(fox_o, fox_onorm).reshape(B, L, FOX_WIDTH) * jax.nn.sigmoid(og)
    mix = jnp.concatenate([go.astype(z.dtype), fo.astype(z.dtype)], axis=-1)
    return mix @ w_out

def peer(x, w_query, sub_keys, expert_u, expert_v):
    shp = x.shape
    xf = x.reshape(-1, D_MODEL)
    T = xf.shape[0]
    nb = -(-T // PEER_BLOCK)
    xb = jnp.pad(xf, ((0, nb * PEER_BLOCK - T), (0, 0))).reshape(nb, PEER_BLOCK, D_MODEL)

    def block(xi):
        qry = (xi @ w_query).reshape(PEER_BLOCK, PEER_HEADS, 2, PEER_HALF)
        s = jnp.einsum('thpc,pnc->thpn', qry, sub_keys, preferred_element_type=jnp.float32)
        s1, i1 = lax.top_k(s[:, :, 0], PEER_TOPK)
        s2, i2 = lax.top_k(s[:, :, 1], PEER_TOPK)
        cand = (s1[..., :, None] + s2[..., None, :]).reshape(PEER_BLOCK, PEER_HEADS, PEER_TOPK * PEER_TOPK)
        cidx = (i1[..., :, None] * PEER_KEYS + i2[..., None, :]).reshape(PEER_BLOCK, PEER_HEADS, PEER_TOPK * PEER_TOPK)
        top_s, pos = lax.top_k(cand, PEER_TOPK)
        idx = jnp.take_along_axis(cidx, pos, axis=-1)
        gate = jax.nn.softmax(top_s, axis=-1)
        hid = jax.nn.gelu(jnp.einsum('td,thkd->thk', xi, expert_u[idx], preferred_element_type=jnp.float32), approximate=False)
        return jnp.einsum('thk,thkd->td', (gate * hid).astype(xi.dtype), expert_v[idx])

    y = lax.map(block, xb).reshape(-1, D_MODEL)[:T]
    return y.reshape(shp)

def setup_inputs(seed: int = 0) -> dict:
    key = jax.random.key(seed)
    ks = jax.random.split(key, 32)
    n_pages = PAST_LEN // PAGE_SIZE
    n_phys = (DEC_BATCH * n_pages * 5) // 4

    def nrm(k, shape, scale):
        return jax.random.normal(k, shape, jnp.float32) * scale

    dt = jnp.exp(jax.random.uniform(ks[13], (DEPTH, GDN_HEADS), minval=float(np.log(1e-3)), maxval=float(np.log(1e-1))))
    return {
        'x_prompt': nrm(ks[0], (BATCH, SEQ, D_MODEL), 1.0),
        'x_sample': nrm(ks[1], (DEC_BATCH, DEC_SEQ, D_MODEL), 1.0),
        'cache_k': nrm(ks[2], (DEPTH, n_phys, PAGE_SIZE, FOX_HEADS, HEAD_DIM), 1.0),
        'cache_v': nrm(ks[3], (DEPTH, n_phys, PAGE_SIZE, FOX_HEADS, HEAD_DIM), 1.0),
        'cache_logf': jax.nn.log_sigmoid(3.0 + nrm(ks[4], (DEPTH, n_phys, PAGE_SIZE, FOX_HEADS), 0.5)),
        'state_gdn': nrm(ks[5], (DEPTH, DEC_BATCH, GDN_HEADS, HEAD_DIM, HEAD_DIM), 0.1),
        'state_conv': nrm(ks[6], (DEPTH, DEC_BATCH, CONV_W - 1, GDN_CONV_DIM), 1.0),
        'page_table': jax.random.permutation(ks[7], n_phys)[:DEC_BATCH * n_pages].reshape(DEC_BATCH, n_pages).astype(jnp.int32),
        'meta_tokens': nrm(ks[8], (N_META, D_MODEL), 1.0),
        'norm_mix': 1.0 + nrm(ks[9], (DEPTH, D_MODEL), 0.02),
        'w_in': nrm(ks[10], (DEPTH, D_MODEL, IN_COLS), D_MODEL ** -0.5),
        'conv_w': nrm(ks[11], (DEPTH, CONV_W, GDN_CONV_DIM), CONV_W ** -0.5),
        'gdn_a_log': jnp.log(jax.random.uniform(ks[12], (DEPTH, GDN_HEADS), minval=1.0, maxval=16.0)),
        'gdn_dt_bias': dt + jnp.log(-jnp.expm1(-dt)),
        'gdn_onorm': 1.0 + nrm(ks[14], (DEPTH, HEAD_DIM), 0.02),
        'fox_f_bias': 3.0 + nrm(ks[15], (DEPTH, FOX_HEADS), 0.5),
        'fox_qnorm': 1.0 + nrm(ks[16], (DEPTH, HEAD_DIM), 0.02),
        'fox_knorm': 1.0 + nrm(ks[17], (DEPTH, HEAD_DIM), 0.02),
        'fox_onorm': 1.0 + nrm(ks[18], (DEPTH, HEAD_DIM), 0.02),
        'w_out': nrm(ks[19], (DEPTH, MIX_WIDTH, D_MODEL), MIX_WIDTH ** -0.5),
        'norm_ffn': 1.0 + nrm(ks[20], (DEPTH, D_MODEL), 0.02),
        'peer_w_query': nrm(ks[21], (DEPTH, D_MODEL, PEER_HEADS * PEER_DKEY), D_MODEL ** -0.5),
        'peer_sub_keys': nrm(ks[22], (DEPTH, 2, PEER_KEYS, PEER_HALF), PEER_HALF ** -0.5),
        'peer_u': nrm(ks[23], (DEPTH, PEER_EXPERTS, D_MODEL), D_MODEL ** -0.5),
        'peer_v': nrm(ks[24], (DEPTH, PEER_EXPERTS, D_MODEL), PEER_HEADS ** -0.5),
    }

def reference(x_prompt, x_sample, cache_k, cache_v, cache_logf, state_gdn, state_conv, page_table,
              meta_tokens, norm_mix, w_in, conv_w, gdn_a_log, gdn_dt_bias, gdn_onorm,
              fox_f_bias, fox_qnorm, fox_knorm, fox_onorm, w_out, norm_ffn,
              peer_w_query, peer_sub_keys, peer_u, peer_v):
    dtype = x_prompt.dtype
    B, S = x_prompt.shape[:2]
    DB, DS = x_sample.shape[:2]
    past_len = page_table.shape[1] * PAGE_SIZE
    hp = jnp.concatenate([jnp.broadcast_to(meta_tokens.astype(dtype)[None], (B, N_META, D_MODEL)), x_prompt], axis=1)
    hs = x_sample
    kp_l, vp_l, fp_l, gp_l, cp_l = [], [], [], [], []
    ks_l, vs_l, fs_l, gs_l, cs_l = [], [], [], [], []
    for l in range(DEPTH):
        qkv_g, a_g, b_g, z_g, qkv_f, f_f, og_f = split_in(rmsnorm(hp, norm_mix[l]) @ w_in[l])
        conv_in = jnp.pad(qkv_g, ((0, 0), (CONV_W - 1, 0), (0, 0)))
        q, k, v, g, beta = gdn_inputs(conv_in, a_g, b_g, conv_w[l], gdn_a_log[l], gdn_dt_bias[l])
        st = jnp.zeros((B, GDN_HEADS, HEAD_DIM, HEAD_DIM), jnp.float32)
        st, o_meta = gdn_chunk(st, q[:, :, :N_META], k[:, :, :N_META], v[:, :, :N_META], g[:, :, :N_META], beta[:, :, :N_META])
        chunks = (to_chunks(q[:, :, N_META:]), to_chunks(k[:, :, N_META:]), to_chunks(v[:, :, N_META:]),
                  to_chunks(g[:, :, N_META:]), to_chunks(beta[:, :, N_META:]))
        st, o_rest = lax.scan(lambda s_, xs: gdn_chunk(s_, *xs), st, chunks)
        o_gdn = jnp.concatenate([o_meta, from_chunks(o_rest)], axis=2)
        fq, fk, fv, logf = fox_inputs(qkv_f, f_f, fox_f_bias[l], fox_qnorm[l], fox_knorm[l])
        o_fox = fox_prompt(fq, jnp.cumsum(logf, axis=1), fk, fv)
        hp = hp + merge_heads(o_gdn, z_g, o_fox, og_f, gdn_onorm[l], fox_onorm[l], w_out[l])
        kp_l.append(fk); vp_l.append(fv); fp_l.append(logf.astype(dtype))
        gp_l.append(st.astype(dtype)); cp_l.append(conv_in[:, -(CONV_W - 1):])

        qkv_gs, a_gs, b_gs, z_gs, qkv_fs, f_fs, og_fs = split_in(rmsnorm(hs, norm_mix[l]) @ w_in[l])
        conv_in_s = jnp.concatenate([state_conv[l].astype(qkv_gs.dtype), qkv_gs], axis=1)
        q, k, v, g, beta = gdn_inputs(conv_in_s, a_gs, b_gs, conv_w[l], gdn_a_log[l], gdn_dt_bias[l])
        st_s, o_gdn_s = gdn_chunk(state_gdn[l].astype(jnp.float32), q, k, v, g, beta)
        fq_s, fk_s, fv_s, logf_s = fox_inputs(qkv_fs, f_fs, fox_f_bias[l], fox_qnorm[l], fox_knorm[l])
        k_past = cache_k[l][page_table].reshape(DB, past_len, FOX_HEADS, HEAD_DIM).astype(fk_s.dtype)
        v_past = cache_v[l][page_table].reshape(DB, past_len, FOX_HEADS, HEAD_DIM).astype(fv_s.dtype)
        c_past = jnp.cumsum(cache_logf[l][page_table].reshape(DB, past_len, FOX_HEADS).astype(jnp.float32), axis=1)
        c_new = c_past[:, -1:] + jnp.cumsum(logf_s, axis=1)
        o_fox_s = fox_attend(fq_s, c_new, past_len + jnp.arange(DS, dtype=jnp.int32),
                             jnp.concatenate([k_past, fk_s], axis=1), jnp.concatenate([v_past, fv_s], axis=1),
                             jnp.concatenate([c_past, c_new], axis=1), jnp.arange(past_len + DS, dtype=jnp.int32))
        hs = hs + merge_heads(o_gdn_s, z_gs, o_fox_s, og_fs, gdn_onorm[l], fox_onorm[l], w_out[l])
        ks_l.append(fk_s); vs_l.append(fv_s); fs_l.append(logf_s.astype(dtype))
        gs_l.append(st_s.astype(dtype)); cs_l.append(conv_in_s[:, -(CONV_W - 1):])

        if l == DEPTH - 1:
            hp = hp[:, N_META:]
        hp = hp + peer(rmsnorm(hp, norm_ffn[l]), peer_w_query[l], peer_sub_keys[l], peer_u[l], peer_v[l])
        hs = hs + peer(rmsnorm(hs, norm_ffn[l]), peer_w_query[l], peer_sub_keys[l], peer_u[l], peer_v[l])
    return (hp, hs,
            jnp.stack(kp_l), jnp.stack(vp_l), jnp.stack(fp_l), jnp.stack(gp_l), jnp.stack(cp_l),
            jnp.stack(ks_l), jnp.stack(vs_l), jnp.stack(fs_l), jnp.stack(gs_l), jnp.stack(cs_l))


_drawn_inputs = setup_inputs


def setup_inputs(seed=0):
    import zlib

    import numpy as np

    out = dict(_drawn_inputs(seed))
    spreads = {}
    factors = {'gdn_onorm': 41.516,
     'fox_qnorm': 3.813,
     'fox_knorm': 2.884,
     'fox_onorm': 46.324,
     'norm_ffn': 17.093}
    for name, (base, spread) in spreads.items():
        noise = np.random.default_rng([zlib.crc32(name.encode()), seed]).standard_normal(out[name].shape)
        drawn = base * np.exp(spread * noise) if base else spread * noise
        out[name] = __import__('jax').numpy.asarray(drawn.astype(out[name].dtype))
    for name, factor in factors.items():
        out[name] = (out[name] * factor).astype(out[name].dtype)
    return out
```

```python
from contextlib import ExitStack

import numpy as np

import concourse.bass as bass
from concourse import mybir

ALU = mybir.AluOpType
ACT = mybir.ActivationFunctionType
AX_X = mybir.AxisListType.X
F32 = mybir.dt.float32
I32 = mybir.dt.int32
U32 = mybir.dt.uint32
ds = bass.ds

P = 128
D = 2048
KT = D // P
HEADS = 8
HD = 128
NB, NQ = 8, 4
NS = NB * NQ
NM = 16
NP = 512
T0 = NS + NM
PT = NP // P
NT = PT + 1
MX = PT
TW = NT * P
NPK = T0 + NP
NY = NS + NP
CONV = 4
PAGES = 16
EPS = 1e-6
TOPK = 16
KEYS = 128
RAWS = NB * (NQ + CONV - 1)
RAWP = CONV - 1 + NM + NP
C_K, C_V, C_A = HEADS * HD, 2 * HEADS * HD, 3 * HEADS * HD
C_Z = C_A + 2 * HEADS
C_FQ = C_Z + HEADS * HD
C_F = C_FQ + 3 * HEADS * HD
C_OG = C_F + HEADS
SCALE = float(HD) ** -0.5
NEG = -1e30
LEVELS = (1, 2, 4, 8, 16, 32, 64)


def constant_parts():
    r = np.arange(P)
    row, col = r[:, None], r[None, :]
    seq0 = np.where(r < NS, r // NQ, np.where(r < T0, NB, -1 - r))
    same0 = (seq0[:, None] == seq0[None, :]) & (r < T0)[:, None]
    upto = [row <= col] * PT + [(row <= col) & same0]
    after = [row > col] * PT + [(row > col) & same0]
    levels = [((row // b) % 2 == 1) & (col // b == row // b - 1) for b in LEVELS]
    parts = {
        "upto": np.concatenate(upto, 1),
        "after": np.concatenate(after, 1),
        "levels": np.concatenate(levels, 1),
        "ident": row == col,
        "ones": np.ones((P, P)),
        "causal": np.where(col > row, NEG, 0.0),
        "causal0": np.where(same0 & (col <= row) | (row >= NS), 0.0, NEG)[:, :NS],
        "members": seq0[:, None] == np.arange(NB + 1)[None, :],
        "batch_cols": np.broadcast_to((np.arange(NS)[None, :] // NQ == np.arange(NB)[:, None]).reshape(1, -1),
                                      (P, NB * NS)),
        "iota": np.broadcast_to(np.arange(TOPK)[None, :], (P, TOPK)),
        "eps": np.full((P, 1), EPS),
        "eps_q": np.full((P, 1), EPS * HD),
        "row": row,
        "fold": (row % NS == np.arange(NS)[None, :]),
    }
    return {k: np.asarray(v, np.float32) for k, v in parts.items()}


def constant_array():
    return np.ascontiguousarray(np.concatenate(list(constant_parts().values()), 1))


def constant_places():
    at, places = 0, {}
    for k, v in constant_parts().items():
        places[k] = (at, at + v.shape[1])
        at += v.shape[1]
    return places, at


class Counter:

    def __init__(self, engine, sem, h, per):
        self.engine, self.sem, self.h, self.per, self.n = engine, sem, h, per, 0

    def link(self, ins):
        self.n += 1
        assert self.n <= self.per, "raise the number of links in a turn"
        ins.then_inc(self.sem, 1)
        self.engine.wait_ge(self.sem, self.h * self.per + self.n)

    def mark(self, ins):
        self.n += 1
        assert self.n <= self.per, "raise the number of links in a turn"
        ins.then_inc(self.sem, 1)

    def wait(self):
        self.engine.wait_ge(self.sem, self.h * self.per + self.n)

    def close(self):
        if self.n < self.per:
            self.engine.sem_inc(self.sem, self.per - self.n)


def build(nc, ins, outs):
    with ExitStack() as ctx:
        places, width = constant_places()
        const = ctx.enter_context(nc.sbuf_tensor("const", [P, width], F32))

        def cst(name, a=0, b=None):
            lo, hi = places[name]
            return const[:, lo + a:(hi if b is None else lo + b)]

        vecs = ctx.enter_context(nc.sbuf_tensor("vecs", [P, V_END], F32))
        mem = {"const": const, "cst": cst, "vecs": vecs}
        scr = {
            "c": nc.dram_tensor("c_scratch", (2, HEADS, TW), F32, kind="Internal").ap(),
            "h": nc.dram_tensor("h_scratch", (NY, D), F32, kind="Internal").ap(),
            "xi": nc.dram_tensor("xi_scratch", (NY, D), F32, kind="Internal").ap(),
        }
        mem["skT"] = ctx.enter_context(nc.sbuf_tensor("skT", [P, 2, KEYS], F32))
        mem["idx_all"] = ctx.enter_context(nc.sbuf_tensor("idx_all", [P, NT, HEADS, TOPK], I32))
        mem["gate_all"] = ctx.enter_context(nc.sbuf_tensor("gate_all", [P, NT, HEADS, TOPK], F32))
        with ExitStack() as mix:
            mem["mixT"] = mix.enter_context(nc.sbuf_tensor("mixT", [P, KT, NY], F32))
            with ExitStack() as front:
                def sb(name, shape, dt=F32):
                    mem[name] = front.enter_context(nc.sbuf_tensor(name, shape, dt))
                sb("xnT", [P, KT, NPK])
                sb("g_all", [P, NT, HEADS])
                sb("beta_all", [P, NT, HEADS])
                sb("logf_all", [P, NT, HEADS])
                sb("logf_past", [P, PAGES, HEADS])
                sb("taps_all", [P, CONV, 3, HEADS])
                sb("page_rows", [P, PAGES])
                norm_and_gates(nc, ins, outs, mem, scr)
                gdn_heads(nc, ins, outs, mem)
                fox_heads(nc, ins, outs, mem, scr)
            with ExitStack() as ffn:
                mem["hres"] = ffn.enter_context(nc.sbuf_tensor("hres", [P, NT, D], F32))
                mix_out(nc, ins, mem)
                mem["xiT"] = mem["mixT"]
                ffn_norm(nc, ins, mem, scr)
            route(nc, ins, mem)
        experts(nc, ins, outs, mem, scr)




POOL_DMA = ("past_in gs_out gp_out cs_out cp_out k_past v_past k_out v_out km_out vm_out ks_out vs_out "
            + " ".join(f"landed{m}" for m in range(16))).split()


def phase(nc, tag, names, sbufs, psums):
    ctx = ExitStack()
    sem = {n: ctx.enter_context(nc.semaphore(f"{tag}_{n}")) for n in names.split() if n not in POOL_DMA}
    numbers = sorted(s.num for s in sem.values())
    sem.update((n, nc.alloc_semaphore(f"{tag}_{n}")) for n in names.split() if n in POOL_DMA)
    starts = [n for n in numbers if n - 1 not in numbers]
    ends = [n + 1 for n in numbers if n + 1 not in numbers]

    def clear():
        for a, b in zip(starts, ends):
            nc.all_engine_barrier(sems_to_clear=range(a, b))

    ctx.callback(clear)
    buf = {}
    for n, (shape, *dt) in sbufs.items():
        buf[n] = ctx.enter_context(nc.sbuf_tensor(f"{tag}_{n}", shape, dt[0] if dt else F32))
    for n, shape in psums.items():
        buf[n] = ctx.enter_context(nc.psum_tensor(f"{tag}_{n}", shape, F32))
    return ctx, sem, buf


V_TAPS = 0
V_MIX = CONV * 3 * HEADS
V_GO, V_FQ, V_FK, V_FO = V_MIX + KT, V_MIX + KT + 1, V_MIX + KT + 2, V_MIX + KT + 3
V_END = V_FO + 1


def rows_of(t):
    return T0 if t == MX else P


def packed(t):
    return t * P, t * P + rows_of(t)


def y_cols(t):
    return t * P, t * P + (NS if t == MX else P)


def norm_and_gates(nc, ins, outs, mem, scr):
    cst, xnT = mem["cst"], mem["xnT"]
    ctx, sem, buf = phase(
        nc, "norm",
        "const_in vec_rows_in narrow_in bias_in pages_in x_in0 x_in1 x_squared x_root x_scaled x_turned "
        "x_evac vec_turned vecs_ready narrow_done narrow_copied gate_order act_order logf_ready c_done c_ready "
        "stored c_stored rows_ready past_in g_ready zeroed logf0_ready",
        {
            "x": ([P, 2, D],), "sq": ([P, D],), "ss": ([P, NT],), "rt": ([P, NT],), "rs": ([P, NT],),
            "vec_rows": ([V_END, P],), "w_narrow": ([P, KT, 24],), "narrow": ([P, NT, 24],),
            "bias": ([P, 3, HEADS],), "af": ([P, NT, 16],), "ab": ([P, NT, 16],), "ea": ([P, HEADS],),
            "logf0": ([P, HEADS],), "cT": ([HEADS, 2, TW],), "pages": ([P, PAGES], I32),
            "rowf": ([P, PAGES],), "rowi": ([P, PAGES], I32),
        },
        {"turn": [P, 4, 512], "nar": [P, NT, 32], "cps": [HEADS, 2, 512], "vps": [P, P]},
    )
    vecs = mem["vecs"]
    with ctx:
        x, sq, ss, rt, rs = buf["x"], buf["sq"], buf["ss"], buf["rt"], buf["rs"]
        turn, nar, cps, vps = buf["turn"], buf["nar"], buf["cps"], buf["vps"]
        narrow, bias, af, ab, ea = buf["narrow"], buf["bias"], buf["af"], buf["ab"], buf["ea"]
        logf0, cT = buf["logf0"], buf["cT"]
        g_all, beta_all, logf_all = mem["g_all"], mem["beta_all"], mem["logf_all"]
        w_in = ins["w_in"][0].rearrange("(k p) c -> p k c", p=P)
        block = ctx.enter_context(nc.Block())

        @block.sync
        def _(sp):
            sp.dma_start(mem["const"][:], ins["constants"]).then_inc(sem["const_in"], 16)
            for r, src in (
                (V_TAPS, ins["conv_w"][0].rearrange("i (s p) -> (i s) p", p=P)),
                (V_MIX, ins["norm_mix"][0].rearrange("(k p) -> k p", p=P)),
                (V_GO, ins["gdn_onorm"]), (V_FQ, ins["fox_qnorm"]), (V_FK, ins["fox_knorm"]), (V_FO, ins["fox_onorm"]),
            ):
                sp.dma_start(buf["vec_rows"][r:r + src.shape[0], :], src).then_inc(sem["vec_rows_in"], 16)
            for t in range(NT):
                if t >= 2:
                    sp.wait_ge(sem["x_turned"], 4 * (t - 1))
                if t == MX:
                    sp.dma_start(x[0:NS, 0, :], ins["x_sample"].rearrange("b q d -> (b q) d")).then_inc(sem["x_in0"], 16)
                    sp.dma_start(x[NS:T0, 0, :], ins["meta_tokens"]).then_inc(sem["x_in0"], 16)
                else:
                    sp.dma_start(x[:, t % 2, :], ins["x_prompt"][0, t * P:(t + 1) * P, :]).then_inc(sem[f"x_in{t % 2}"], 16)
                if t == 1:
                    sp.dma_start(buf["w_narrow"][:, :, 0:16], w_in[:, :, C_A:C_Z]).then_inc(sem["narrow_in"], 16)
                    sp.dma_start(buf["w_narrow"][:, :, 16:24], w_in[:, :, C_F:C_OG]).then_inc(sem["narrow_in"], 16)
                    for i, n in enumerate(("gdn_dt_bias", "fox_f_bias", "gdn_a_log")):
                        sp.dma_start(bias[:, i, :], ins[n][0].partition_broadcast(P)).then_inc(sem["bias_in"], 16)
                    sp.dma_start(buf["pages"][:], ins["page_table"].rearrange("b n -> (b n)").partition_broadcast(P)
                                 ).then_inc(sem["pages_in"], 16)
            sp.wait_ge(sem["logf_ready"], 1)
            lp = outs["logf_prompt"][0, 0]
            sp.dma_start(outs["logf_sample"][0].rearrange("b q h -> (b q) h"), logf_all[0:NS, MX, :]).then_inc(sem["stored"], 16)
            sp.dma_start(lp[0:NM, :], logf_all[NS:T0, MX, :]).then_inc(sem["stored"], 16)
            sp.dma_start(lp[NM:, :].rearrange("(t p) h -> p t h", p=P), logf_all[:, 0:PT, :]).then_inc(sem["stored"], 16)
            sp.wait_ge(sem["c_ready"], 2)
            sp.dma_start(scr["c"].rearrange("s h t -> h s t"), cT[:]).then_inc(sem["c_stored"], 16)
            sp.wait_ge(sem["stored"], 48)
            sp.wait_ge(sem["c_stored"], 16)

        @block.gpsimd
        def _(pool):
            pool.wait_ge(sem["rows_ready"], 3)
            for n in range(PAGES):
                pool.indirect_dma_start(mem["logf_past"][:, n, :], None, ins["cache_logf"][0].rearrange("n p h -> (n p) h"),
                                        bass.IndirectOffsetOnAxis(ap=buf["rowi"][:, n:n + 1], axis=0)
                                        ).then_inc(sem["past_in"], 16)
            pool.wait_ge(sem["past_in"], 16 * PAGES)

        @block.scalar
        def _(act):
            act.wait_ge(sem["const_in"], 16)
            for t in range(NT):
                r = rows_of(t)
                act.wait_ge(sem[f"x_in{t % 2}"], 16 * (t // 2 + (2 if t == MX else 1)))
                nc.scalar.activation(sq[0:r, :], x[0:r, t % 2, :], ACT.Square, accum_out=ss[0:r, t:t + 1]
                                     ).then_inc(sem["x_squared"], 1)
                act.wait_ge(sem["x_squared"], t + 1)
                nc.scalar.activation(rt[0:r, t:t + 1], ss[0:r, t:t + 1], ACT.Sqrt, scale=1.0 / D,
                                     bias=cst("eps")[0:r, :]).then_inc(sem["x_root"], 1)
            act.wait_ge(sem["gate_order"], 3)
            nc.scalar.activation(ab[:], ab[:], ACT.Exp).then_inc(sem["act_order"], 1)
            nc.scalar.activation(ea[:], bias[:, 2, :], ACT.Exp).then_inc(sem["act_order"], 1)
            nc.scalar.activation(beta_all[:], narrow[:, :, 8:16], ACT.Tanh, scale=0.5).then_inc(sem["act_order"], 1)
            act.wait_ge(sem["act_order"], 1)
            nc.scalar.activation(ab[:], ab[:], ACT.Ln, bias=1.0).then_inc(sem["act_order"], 1)

        @block.vector
        def _(dve):
            order = Counter(dve, sem["gate_order"], 0, 16)
            nc.vector.memset(narrow[:], 0.0).then_inc(sem["zeroed"], 1)
            dve.wait_ge(sem["vec_turned"], 1)
            nc.vector.tensor_copy(vecs[:], vps[:, 0:V_END]).then_inc(sem["vecs_ready"], 1)
            dve.wait_ge(sem["vecs_ready"], 1)
            nc.vector.tensor_scalar(mem["taps_all"][:], vecs[:, V_TAPS:V_MIX].rearrange("p (i s h) -> p i s h", i=CONV, s=3),
                                    0.5, None, ALU.mult).then_inc(sem["vecs_ready"], 1)
            dve.wait_ge(sem["pages_in"], 16)
            nc.vector.tensor_copy(buf["rowf"][:], buf["pages"][:]).then_inc(sem["rows_ready"], 1)
            dve.wait_ge(sem["rows_ready"], 1)
            nc.vector.tensor_scalar(buf["rowf"][:], buf["rowf"][:], float(P), cst("row"), ALU.mult, ALU.add
                                    ).then_inc(sem["rows_ready"], 1)
            dve.wait_ge(sem["rows_ready"], 2)
            nc.vector.tensor_copy(buf["rowi"][:], buf["rowf"][:]).then_inc(sem["rows_ready"], 1)
            nc.vector.tensor_scalar(mem["page_rows"][:], buf["rowf"][:], float(HEADS), None, ALU.mult
                                    ).then_inc(sem["rows_ready"], 1)
            for t in range(NT):
                r = rows_of(t)
                a, b = packed(t)
                dve.wait_ge(sem["x_root"], t + 1)
                nc.vector.reciprocal(rs[0:r, t:t + 1], rt[0:r, t:t + 1]).then_inc(sem["x_scaled"], 1)
                dve.wait_ge(sem["x_scaled"], 2 * t + 1)
                nc.vector.tensor_scalar(x[0:r, t % 2, :], x[0:r, t % 2, :], rs[0:r, t:t + 1], None, ALU.mult
                                        ).then_inc(sem["x_scaled"], 1)
                for g in range(4):
                    dve.wait_ge(sem["x_turned"], 4 * t + g + 1)
                    gain = vecs[:, V_MIX + 4 * g:V_MIX + 4 * g + 4].unsqueeze(2).to_broadcast([P, 4, r])
                    nc.vector.tensor_tensor(xnT[:, 4 * g:4 * g + 4, a:b],
                                            turn[:, g, :].rearrange("p (k t) -> p k t", k=4)[:, :, 0:r], gain,
                                            ALU.mult).then_inc(sem["x_evac"], 1)
            dve.wait_ge(sem["narrow_done"], 1)
            dve.wait_ge(sem["zeroed"], 1)
            nc.vector.tensor_copy(narrow[0:T0, MX, :], nar[0:T0, MX, 0:24]).then_inc(sem["narrow_copied"], 1)
            nc.vector.tensor_copy(narrow[:, 0:PT, :], nar[:, 0:PT, 0:24]).then_inc(sem["narrow_copied"], 1)
            dve.wait_ge(sem["narrow_copied"], 2)
            dve.wait_ge(sem["bias_in"], 48)
            for i, c in ((0, 0), (1, 16)):
                order.link(nc.vector.tensor_tensor(af[:, :, 8 * i:8 * i + 8], narrow[:, :, c:c + 8],
                                                   bias[:, i, :].unsqueeze(1).to_broadcast([P, NT, 8]), ALU.add))
            order.link(nc.vector.scalar_tensor_tensor(ab[:], af[:], -1.0, af[:], ALU.mult, ALU.min))
            dve.wait_ge(sem["act_order"], 4)
            order.link(nc.vector.scalar_tensor_tensor(g_all[:], af[:, :, 0:8], 0.0, ab[:, :, 0:8], ALU.max, ALU.add))
            nc.vector.scalar_tensor_tensor(g_all[:], g_all[:], -1.0, ea[:].unsqueeze(1).to_broadcast([P, NT, 8]),
                                           ALU.mult, ALU.mult).then_inc(sem["g_ready"], 1)
            nc.vector.tensor_scalar(beta_all[:], beta_all[:], 0.5, 0.5, ALU.mult, ALU.add).then_inc(sem["g_ready"], 1)
            nc.vector.scalar_tensor_tensor(logf_all[:], af[:, :, 8:16], 0.0, ab[:, :, 8:16], ALU.min, ALU.subtract
                                           ).then_inc(sem["logf_ready"], 1)
            dve.wait_ge(sem["logf_ready"], 1)
            nc.vector.tensor_scalar(logf0[:], logf_all[:, MX, :], cst("members", NB, NB + 1), None, ALU.mult
                                    ).then_inc(sem["logf0_ready"], 1)
            dve.wait_ge(sem["c_done"], 1)
            cflat = cps[:].rearrange("h a b -> h (a b)")[:, 0:TW]
            nc.vector.tensor_copy(cT[:, 0, :], cflat).then_inc(sem["c_ready"], 1)
            nc.vector.tensor_scalar(cT[:, 1, :], cflat, -1.0, None, ALU.mult).then_inc(sem["c_ready"], 1)

        @block.tensor
        def _(pe):
            pe.wait_ge(sem["const_in"], 16)
            pe.wait_ge(sem["vec_rows_in"], 96)
            nc.tensor.transpose(vps[:, 0:V_END], buf["vec_rows"][:], cst("ident")[0:V_END, 0:V_END]
                                ).then_inc(sem["vec_turned"], 1)
            for t in range(NT):
                r = rows_of(t)
                pe.wait_ge(sem["x_scaled"], 2 * t + 2)
                for g in range(4):
                    if t >= 1:
                        pe.wait_ge(sem["x_evac"], 4 * (t - 1) + g + 1)
                    for k in range(4):
                        last = nc.tensor.transpose(turn[:, g, k * P:k * P + r],
                                                   x[0:r, t % 2, (4 * g + k) * P:(4 * g + k + 1) * P],
                                                   cst("ident")[0:r, 0:r])
                    last.then_inc(sem["x_turned"], 1)
            pe.wait_ge(sem["narrow_in"], 32)
            pe.wait_ge(sem["x_evac"], 4 * NT)
            for t in range(NT):
                a, b = packed(t)
                for k in range(KT):
                    last = nc.tensor.matmul(nar[0:b - a, t, 0:24], xnT[:, k, a:b], buf["w_narrow"][:, k, :],
                                            start=(k == 0), stop=(k == KT - 1))
            last.then_inc(sem["narrow_done"], 1)
            pe.wait_ge(sem["logf0_ready"], 1)
            for t in range(NT):
                out = cps[:, t // 4, (t % 4) * P:(t % 4 + 1) * P]
                nc.tensor.matmul(out, logf_all[:, t, :], cst("upto", t * P, (t + 1) * P), start=True, stop=(t == MX))
                for j in range(t % MX):
                    nc.tensor.matmul(out, logf_all[:, j, :], cst("ones"), start=False, stop=False)
                if t != MX:
                    nc.tensor.matmul(out, logf0[:], cst("ones"), start=False, stop=True)
            nc.tensor.matmul(vps[0:HEADS, 0:P], logf0[:], cst("ones"), start=True, stop=True).then_inc(sem["c_done"], 1)


def alone(engine, sem):
    engine.sem_inc(sem, 1)


SEGS = 4


def load_weights(sp, sem, w, w_in, bases, h):
    for s, base in enumerate(bases):
        sp.wait_ge(sem[f"projected{s}"], h + 1)
        sp.dma_start(w[:, s], w_in[:, :, ds(h * HD + base, HD)]).then_inc(sem[f"w_in{s}"], 16)


def project(nc, pe, sem, w, pj, xnT, s, h, steps=(0, KT)):
    r = s % 2
    if steps[0] == 0:
        pe.wait_ge(sem[f"w_in{s}"], (h + 1) * 16)
        pe.wait_ge(sem[f"evacuated{r}"], h * 2 + (s // 2 + 1))
    for k in range(*steps):
        for a, b in ((0, NP), (NP, NPK)):
            last = nc.tensor.matmul(pj[r][:, a:b], w[:, s, k, :], xnT[:, k, a:b], start=(k == 0), stop=(k == KT - 1))
    if steps[1] == KT:
        last.then_inc(sem[f"projected{s}"], 1)


class Ahead:

    def __init__(self, next_head, count, *operands):
        self.next_head, self.steps, self.operands, self.done = next_head, count * KT, operands, 0

    def take(self, steps):
        while self.next_head is not None and steps > 0 and self.done < self.steps:
            s, k = divmod(self.done, KT)
            piece = min(steps, KT - k)
            project(*self.operands, s, self.next_head, (k, k + piece))
            self.done += piece
            steps -= piece

    def finish(self):
        self.take(self.steps)


PROJECT_SEMS = " ".join(f"w_in{s} projected{s}" for s in range(SEGS)) + " evacuated0 evacuated1 "


def gdn_heads(nc, ins, outs, mem):
    cst, xnT, vecs, mixT = mem["cst"], mem["xnT"], mem["vecs"], mem["mixT"]
    ctx, sem, buf = phase(
        nc, "gdn",
        PROJECT_SEMS + "state_in history_in turn_done cleared dve_order act_order pool_order "
        "history_turned history_copied gU_ready after_sums upto_done decay_done sums_done tails_done "
        "decayT_exp upto_exp decay_exp tails_exp convolved tanh_y silu_done squared squares_done root_q root_k inverted "
        "qk_ready grown gate_ready tanh_z v_turned v_copied k_turned kN_ready kk_done qk_done A_ready PT_ready "
        "masked_decay masked_decayT M_ready X_ready XT_turned XT_copied QT_done QT_copied Y_done YT_done XT_ready "
        "grown_apart ks_done w_ready u_done u_copied um_ready ds_done S_ready o_done o_squared "
        "o_sums o_root oN_ready oT_done u_apart dss_done scaled_state state_out_ready rows_compact rows_turned "
        "rows_ready stores_done gs_out gp_out cs_out cp_out pe_passed pool_passed",
        {
            "w": ([P, SEGS, KT, HD],), "raw": ([P, 3, RAWS + RAWP],), "y": ([P, 3, NPK],), "th": ([P, 3, TW],),
            "qkvT": ([P, 3, TW],), "zT": ([P, NY],), "gz": ([P, NY],),
            "hist": ([NB * 3, 3, HD],), "state": ([P, NB, HD],), "sout": ([P, NB, HD],),
            "gcol": ([P, NT],), "bcol": ([P, NT],), "tap": ([P, CONV, 3],), "gU": ([P, NT, P],), "gsel": ([P, NB + PT],),
            "ET": ([P, NT, P],), "EN": ([P, NT, P],), "eG": ([P, TW],), "tails": ([P, 20],),
            "qke": ([P, 2, TW],), "apart": ([P, 2, NB, NS],),
            "kN": ([P, NT, HD],), "vN": ([P, NT, HD],), "X": ([P, NT, P],), "XT": ([P, NT, P],),
            "QT": ([P, NT, P],), "M": ([P, 2, NT, P],), "uN": ([P, NT, HD],), "um": ([P, HD],),
            "S": ([P, 2, HD],), "ub": ([P, NB, HD],),
            "oms": ([P, NT],), "ort": ([P, NT],), "ors": ([P, NT],),
            "rowc": ([P, 3, 27],), "rowN": ([27, 3, HD],),
        },
        {"pj0": [P, 1024], "pj1": [P, 1024], "R1": [P, 1024], "R2": [P, 1024]},
    )
    buf.update(sq=buf["qke"], root=buf["th"], A=buf["EN"], sqo=buf["QT"], oN=buf["M"][:, 0])
    B = type("Buffers", (), buf)
    pj, R1, R2 = (B.pj0, B.pj1), B.R1, B.R2
    w_in = ins["w_in"][0].rearrange("(k p) c -> p k c", p=P)
    LV = len(LEVELS) - 1
    AHEAD = 3

    def tiles(region):
        return region[:, 0:TW].rearrange("p (t c) -> p t c", t=NT)

    def wide(tile):
        return tile[:].rearrange("p t c -> p (t c)")

    def cols(tile_cols, width=P):
        return tile_cols[:].unsqueeze(2).to_broadcast([P, NT, width])

    with ctx:
        block = ctx.enter_context(nc.Block())

        @block.sync
        def _(sp):
            with sp.Fori(0, HEADS) as h:
                load_weights(sp, sem, B.w, w_in, (0, C_K, C_V, C_Z), h)
                sp.wait_ge(sem["turn_done"], h + 1)
                sp.dma_start(B.state[:], ins["state_gdn"][0].rearrange("b h k v -> h k b v")[ds(h, 1)].squeeze(0)
                             ).then_inc(sem["state_in"], 16)
                sp.dma_start(B.hist[:], ins["state_conv"][0].rearrange("b i (s c) -> (b i) s c", s=3)[:, :, ds(h * HD, HD)]
                             ).then_inc(sem["history_in"], 16)

        @block.tensor
        def _(pe):
            for s in range(SEGS):
                pe.sem_inc(sem[f"projected{s}"], 1)

            def attend(h, ahead):
                n = h + 1
                ident, ones = cst("ident"), cst("ones")

                def tcst(name, t):
                    return cst(name, t * P, (t + 1) * P)

                pe.wait_ge(sem["turn_done"], n)
                pe.wait_ge(sem["history_in"], n * 16)
                alone(pe, sem["pe_passed"])
                for s in range(3):
                    last = nc.tensor.transpose(R1[:, 32 * s:32 * s + 24], B.hist[:, s, :], ident[0:24, 0:24])
                last.then_inc(sem["history_turned"], 1)
                pe.wait_ge(sem["gU_ready"], n)
                nc.tensor.matmul(R2[:, 0:NP], tcst("after", 0), B.gU[:, 0:PT, :].rearrange("p t c -> p (t c)"),
                                 start=True, stop=True)
                nc.tensor.matmul(R2[:, NP:TW], tcst("after", MX), B.gU[:, MX, :], start=True, stop=True
                                 ).then_inc(sem["after_sums"], 1)
                pe.wait_ge(sem["history_copied"], n)
                nc.tensor.matmul(R1[:, 0:NP], ones, B.gU[:, 0:PT, :].rearrange("p t c -> p (t c)"), start=True, stop=True)
                nc.tensor.matmul(R1[:, NP:TW], ones, B.gU[:, MX, :], start=True, stop=True).then_inc(sem["upto_done"], 1)
                pe.wait_ge(sem["decayT_exp"], n)
                for t in range(NT):
                    last = nc.tensor.matmul(R2[:, t * P:(t + 1) * P], B.gU[:, t, :], tcst("after", t), start=True, stop=True)
                last.then_inc(sem["decay_done"], 1)
                pe.wait_ge(sem["upto_exp"], n)
                for t in range(NT):
                    nc.tensor.matmul(R1[:, t:t + 1], tcst("after", t), B.gcol[:, t:t + 1], start=True, stop=True)
                nc.tensor.matmul(R1[:, 8:8 + NB + PT], ones, B.gsel[:], start=True, stop=True).then_inc(sem["tails_done"], 1)
                pe.wait_ge(sem["rows_compact"], n)
                for s in range(3):
                    last = nc.tensor.transpose(R1[0:27, 512 + s * HD:512 + (s + 1) * HD], B.rowc[:, s, :], ident)
                last.then_inc(sem["rows_turned"], 1)
                project(nc, pe, sem, B.w, pj, xnT, 3, h)
                ahead.take(16)
                pe.wait_ge(sem["squared"], n)
                pe.wait_ge(sem["decay_exp"], n)
                for a, b in ((0, NP), (NP, TW)):
                    last = nc.tensor.matmul(R2[:, a:b], ones, B.sq[:, 0, a:b], start=True, stop=True)
                last.then_inc(sem["squares_done"], 1)
                pe.wait_ge(sem["tails_exp"], n)
                pe.wait_ge(sem["rows_ready"], n)
                for a, b in ((0, NP), (NP, TW)):
                    last = nc.tensor.matmul(R1[:, a:b], ones, B.sq[:, 1, a:b], start=True, stop=True)
                last.then_inc(sem["sums_done"], 1)
                ahead.take(2)
                pe.wait_ge(sem["root_q"], n)
                for t in range(NT):
                    last = nc.tensor.transpose(R2[:, t * P:(t + 1) * P], B.qkvT[:, 2, t * P:(t + 1) * P], ident)
                last.then_inc(sem["v_turned"], 1)
                ahead.take(3)
                pe.wait_ge(sem["root_k"], n)
                pe.wait_ge(sem["qk_ready"], n)
                for t in range(NT):
                    last = nc.tensor.transpose(R1[:, t * P:(t + 1) * P], B.qkvT[:, 1, t * P:(t + 1) * P], ident)
                last.then_inc(sem["k_turned"], 1)
                pe.wait_ge(sem["v_copied"], n)
                for t in range(NT):
                    c = slice(t * P, (t + 1) * P)
                    last = nc.tensor.matmul(R2[:, c], B.qkvT[:, 1, c], B.qkvT[:, 0, c], start=True, stop=True)
                last.then_inc(sem["qk_done"], 1)
                pe.wait_ge(sem["kN_ready"], n)
                for t in range(NT):
                    c = slice(t * P, (t + 1) * P)
                    last = nc.tensor.matmul(R1[:, c], B.qkvT[:, 1, c], B.qkvT[:, 1, c], start=True, stop=True)
                last.then_inc(sem["kk_done"], 1)
                pe.wait_ge(sem["X_ready"], h * (LV + 1) + 1)
                for t in range(NT):
                    last = nc.tensor.transpose(R1[:, t * P:(t + 1) * P], B.X[:, t, :], ident)
                last.then_inc(sem["XT_turned"], 1)
                pe.wait_ge(sem["PT_ready"], n)
                for l in range(1, LV + 1):
                    ahead.take(1)
                    pe.wait_ge(sem["M_ready"], h * LV + l)
                    pe.wait_ge(sem["XT_ready"], h * (LV + 1) + l)
                    for t in range(NT):
                        last = nc.tensor.matmul(R1[:, t * P:(t + 1) * P], B.M[:, l % 2, t, :], B.XT[:, t, :], start=True, stop=True)
                    last.then_inc(sem["QT_done"], 1)
                    ahead.take(1)
                    pe.wait_ge(sem["QT_copied"], h * LV + l)
                    pe.wait_ge(sem["X_ready"], h * (LV + 1) + l)
                    for t in range(NT):
                        last = nc.tensor.matmul(R1[:, t * P:(t + 1) * P], B.X[:, t, :], B.QT[:, t, :], start=True, stop=True)
                    last.then_inc(sem["YT_done"], 1)
                    if l < LV:
                        for t in range(NT):
                            last = nc.tensor.matmul(R2[:, t * P:(t + 1) * P], B.QT[:, t, :], B.X[:, t, :], start=True, stop=True)
                        last.then_inc(sem["Y_done"], 1)
                pe.wait_ge(sem["XT_ready"], h * (LV + 1) + LV + 1)
                pe.wait_ge(sem["grown_apart"], n)
                pe.wait_ge(sem["state_in"], n * 16)
                for b in range(NB):
                    last = nc.tensor.matmul(R1[0:NS, 0:HD], B.apart[:, 1, b, :], B.state[:, b, :], start=(b == 0), stop=(b == NB - 1))
                last.then_inc(sem["ks_done"], 1)

                def values(i, t):
                    ahead.take(1)
                    pe.wait_ge(sem["w_ready"], h * NT + i)
                    nc.tensor.matmul(R1[:, 512 + (i % 2) * HD:512 + (i % 2 + 1) * HD], B.XT[:, t, :], B.vN[:, t, :],
                                     start=True, stop=True).then_inc(sem["u_done"], 1)
                    ahead.take(1)
                    pe.wait_ge(sem["u_copied"], h * NT + i)

                values(1, MX)
                pe.wait_ge(sem["um_ready"], n)
                nc.tensor.matmul(R1[:, 768:896], B.kN[:, MX, :], B.um[:], start=True, stop=True).then_inc(sem["ds_done"], 1)
                nc.tensor.matmul(R2[0:NS, NP:TW], B.ET[:, MX, 0:NS], B.uN[:, MX, :], start=True, stop=False)
                for b in range(NB):
                    last = nc.tensor.matmul(R2[0:NS, NP:TW], B.apart[:, 0, b, :], B.state[:, b, :], start=False, stop=(b == NB - 1))
                last.then_inc(sem["o_done"], 1)
                for t in range(PT):
                    c = slice(t * P, (t + 1) * P)
                    S = B.S[:, t % 2, :]
                    pe.wait_ge(sem["S_ready"], h * NT + t + 1)
                    nc.tensor.matmul(R1[:, c], B.qke[:, 1, c], S, start=True, stop=True).then_inc(sem["ks_done"], 1)
                    values(t + 2, t)
                    nc.tensor.matmul(R1[:, 768:896], B.kN[:, t, :], B.uN[:, t, :],
                                     start=True, stop=True).then_inc(sem["ds_done"], 1)
                    nc.tensor.matmul(R2[:, c], B.qke[:, 0, c], S, start=True, stop=False)
                    nc.tensor.matmul(R2[:, c], B.ET[:, t, :], B.uN[:, t, :], start=False, stop=True).then_inc(sem["o_done"], 1)
                pe.wait_ge(sem["u_apart"], n)
                pe.wait_ge(sem["S_ready"], n * NT)
                for i in range(2):
                    last = nc.tensor.matmul(R1[:, i * 512:(i + 1) * 512], B.kN[:, MX, :],
                                            B.ub[:, 4 * i:4 * i + 4, :].rearrange("p b v -> p (b v)"), start=True, stop=True)
                last.then_inc(sem["dss_done"], 1)
                pe.wait_ge(sem["oN_ready"], n)
                for t in range(NT):
                    a, b = y_cols(t)
                    last = nc.tensor.transpose(R2[:, a:b], B.oN[0:b - a, t, :], ident[0:b - a, 0:b - a])
                last.then_inc(sem["oT_done"], 1)

            def head(h, ahead):
                attend(h, ahead)
                ahead.finish()

            for s in range(AHEAD):
                project(nc, pe, sem, B.w, pj, xnT, s, 0)
            with pe.Fori(0, HEADS - 1) as h:
                head(h, Ahead(h + 1, AHEAD, nc, pe, sem, B.w, pj, xnT))
            head(HEADS - 1, Ahead(None, AHEAD))

        @block.scalar
        def _(act):
            for r in range(2):
                act.sem_inc(sem[f"evacuated{r}"], 1)

            def evacuate(h, segments):
                for s in segments:
                    q = pj[s % 2]
                    act.wait_ge(sem[f"projected{s}"], h + 2)
                    if s == 0:
                        act.wait_ge(sem["convolved"], h + 1)
                    nc.scalar.copy(B.raw[:, s, 0:RAWS].rearrange("p (b j) -> p b j", b=NB)[:, :, CONV - 1:],
                                   q[:, NP:NP + NS].rearrange("p (b j) -> p b j", b=NB))
                    nc.scalar.copy(B.raw[:, s, RAWS + CONV - 1:RAWS + CONV - 1 + NM], q[:, NP + NS:NPK])
                    nc.scalar.copy(B.raw[:, s, RAWS + CONV - 1 + NM:], q[:, 0:NP]).then_inc(sem[f"evacuated{s % 2}"], 1)

            def evacuate_gate(h):
                act.wait_ge(sem["projected3"], h + 2)
                act.wait_ge(sem["gate_ready"], h + 1)
                nc.scalar.mul(B.zT[:], pj[1][:, 0:NY], 0.5).then_inc(sem["evacuated1"], 1)

            def attend(h, last):
                n = h + 1
                act.wait_ge(sem["turn_done"], n)
                act.wait_ge(sem["after_sums"], n)
                nc.scalar.activation(wide(B.ET), R2[:, 0:TW], ACT.Exp).then_inc(sem["decayT_exp"], 1)
                act.wait_ge(sem["upto_done"], n)
                nc.scalar.activation(B.eG[:], R1[:, 0:TW], ACT.Exp).then_inc(sem["upto_exp"], 1)
                act.wait_ge(sem["decay_done"], n)
                nc.scalar.activation(wide(B.EN), R2[:, 0:TW], ACT.Exp).then_inc(sem["decay_exp"], 1)
                act.wait_ge(sem["tails_done"], n)
                nc.scalar.activation(B.tails[:, 0:NT], R1[:, 0:NT], ACT.Exp).then_inc(sem["act_order"], 1)
                nc.scalar.activation(B.tails[:, 8:20], R1[:, 8:20], ACT.Exp).then_inc(sem["tails_exp"], 1)
                evacuate_gate(h)
                act.wait_ge(sem["evacuated1"], h * 2 + 3)
                nc.scalar.activation(B.gz[:], B.zT[:], ACT.Tanh).then_inc(sem["tanh_z"], 1)
                act.wait_ge(sem["convolved"], n + 1)
                nc.scalar.activation(B.th[:, :, 0:NPK], B.y[:], ACT.Tanh).then_inc(sem["tanh_y"], 1)
                act.wait_ge(sem["silu_done"], n)
                nc.scalar.activation(B.sq[:], B.qkvT[:, 0:2, :], ACT.Square).then_inc(sem["squared"], 1)
                act.wait_ge(sem["squares_done"], n)
                nc.scalar.activation(B.root[:, 0, :], R2[:, 0:TW], ACT.Ln, scale=float(HD), bias=cst("eps_q")
                                     ).then_inc(sem["root_q"], 1)
                act.wait_ge(sem["sums_done"], n)
                nc.scalar.activation(B.root[:, 1, :], R1[:, 0:TW], ACT.Ln, bias=cst("eps")).then_inc(sem["root_k"], 1)
                act.wait_ge(sem["root_q"], n)
                act.wait_ge(sem["root_k"], n)
                nc.scalar.activation(B.root[:, 0:2, :], B.root[:, 0:2, :], ACT.Exp, scale=-0.5).then_inc(sem["inverted"], 1)
                act.wait_ge(sem["v_turned"], n)
                nc.scalar.copy(wide(B.vN), R2[:, 0:TW]).then_inc(sem["v_copied"], 1)
                act.wait_ge(sem["XT_turned"], n)
                nc.scalar.copy(wide(B.XT), R1[:, 0:TW]).then_inc(sem["XT_ready"], 1)
                for l in range(1, LV + 1):
                    act.wait_ge(sem["QT_done"], h * LV + l)
                    nc.scalar.copy(wide(B.QT), R1[:, 0:TW]).then_inc(sem["QT_copied"], 1)
                if not last:
                    evacuate(h + 1, (0,))
                for i, t in enumerate((MX, *range(PT))):
                    act.wait_ge(sem["u_done"], h * NT + i + 1)
                    nc.scalar.copy(B.uN[:, t, :], R1[:, 512 + ((i + 1) % 2) * HD:512 + ((i + 1) % 2 + 1) * HD]
                                   ).then_inc(sem["u_copied"], 1)
                act.wait_ge(sem["o_done"], n * NT)
                nc.scalar.activation(wide(B.sqo), R2[:, 0:TW], ACT.Square).then_inc(sem["o_squared"], 1)
                act.wait_ge(sem["o_sums"], n)
                nc.scalar.activation(B.ort[:], B.oms[:], ACT.Sqrt, scale=1.0 / HD, bias=cst("eps")).then_inc(sem["o_root"], 1)

            def head(h, last):
                evacuate(h, (1, 2))
                attend(h, last)

            evacuate(0, (0,))
            with act.Fori(0, HEADS - 1) as h:
                head(h, False)
            head(HEADS - 1, True)

        @block.vector
        def _(dve):
            nc.vector.memset(B.qkvT[:], 0.0).then_inc(sem["cleared"], 1)
            nc.vector.memset(B.raw[:], 0.0).then_inc(sem["cleared"], 1)
            dve.wait_ge(sem["cleared"], 2)
            dve.sem_inc(sem["convolved"], 1)
            dve.sem_inc(sem["gate_ready"], 1)
            dve.sem_inc(sem["turn_done"], 1)

            def attend(h):
                n = h + 1
                order = Counter(dve, sem["dve_order"], h, 60)
                dve.wait_ge(sem["stores_done"], n)
                order.mark(nc.vector.tensor_copy(B.gcol[:], mem["g_all"][:, :, ds(h, 1)].rearrange("p t o -> p (t o)")))
                order.mark(nc.vector.tensor_copy(B.bcol[:], mem["beta_all"][:, :, ds(h, 1)].rearrange("p t o -> p (t o)")))
                order.mark(nc.vector.tensor_copy(B.tap[:], mem["taps_all"][:, :, :, ds(h, 1)].rearrange("p i s o -> p i (s o)")))
                order.wait()
                order.mark(nc.vector.tensor_scalar(B.gsel[:, 0:NB], cst("members", 0, NB), B.gcol[:, MX:MX + 1], None, ALU.mult))
                order.mark(nc.vector.tensor_copy(B.gsel[:, NB:], B.gcol[:, 0:PT]))
                nc.vector.tensor_tensor(B.gU[:], cst("upto").rearrange("p (t c) -> p t c", t=NT), cols(B.gcol), ALU.mult
                                        ).then_inc(sem["gU_ready"], 1)
                dve.wait_ge(sem["history_turned"], n)
                for s in range(3):
                    last = nc.vector.tensor_copy(B.raw[:, s, 0:RAWS].rearrange("p (b j) -> p b j", b=NB)[:, :, 0:CONV - 1],
                                                 R1[:, 32 * s:32 * s + 24].rearrange("p (b i) -> p b i", b=NB))
                last.then_inc(sem["history_copied"], 1)
                dve.wait_ge(sem["history_copied"], n)
                for r in range(2):
                    dve.wait_ge(sem[f"evacuated{r}"], h * 2 + (3 if r == 0 else 2))
                for s in range(3):
                    order.mark(nc.vector.tensor_copy(
                        B.rowc[:, s, 0:24].rearrange("p (b i) -> p b i", b=NB),
                        B.raw[:, s, 0:RAWS].rearrange("p (b j) -> p b j", b=NB)[:, :, NQ:]))
                nc.vector.tensor_copy(B.rowc[:, :, 24:27], B.raw[:, :, RAWS + RAWP - 3:]).then_inc(sem["rows_compact"], 1)
                for i in range(CONV):
                    for s in range(3):
                        parts = (
                            (B.y[:, s, NS:], B.raw[:, s, RAWS + i:RAWS + i + NM + NP]),
                            (B.y[:, s, 0:NS].rearrange("p (b q) -> p b q", b=NB),
                             B.raw[:, s, 0:RAWS].rearrange("p (b j) -> p b j", b=NB)[:, :, i:i + NQ]),
                        )
                        for y, raw in parts:
                            tap = B.tap[:, i, s:s + 1]
                            if i == 0:
                                last = nc.vector.tensor_scalar(y, raw, tap, None, ALU.mult)
                            else:
                                last = nc.vector.scalar_tensor_tensor(y, raw, tap, y, ALU.mult, ALU.add)
                            if i < CONV - 1 or s < 2 or y is parts[0][0]:
                                order.mark(last)
                            else:
                                last.then_inc(sem["convolved"], 1)
                    if i < CONV - 1:
                        order.wait()
                dve.wait_ge(sem["tanh_z"], n)
                nc.vector.scalar_tensor_tensor(B.gz[:], B.gz[:], 1.0, B.zT[:], ALU.add, ALU.mult).then_inc(sem["gate_ready"], 1)
                dve.wait_ge(sem["tanh_y"], n)
                order.mark(nc.vector.scalar_tensor_tensor(B.qkvT[:, :, NP:NPK], B.th[:, :, 0:T0], 1.0, B.y[:, :, 0:T0],
                                                          ALU.add, ALU.mult))
                nc.vector.scalar_tensor_tensor(B.qkvT[:, :, 0:NP], B.th[:, :, T0:NPK], 1.0, B.y[:, :, T0:], ALU.add, ALU.mult
                                               ).then_inc(sem["silu_done"], 1)
                dve.wait_ge(sem["rows_turned"], n)
                nc.vector.tensor_copy(B.rowN[:], R1[0:27, 512:512 + 3 * HD].rearrange("p (s c) -> p s c", s=3)
                                      ).then_inc(sem["rows_ready"], 1)
                dve.wait_ge(sem["inverted"], n)
                dve.wait_ge(sem["silu_done"], n)
                nc.vector.tensor_tensor(B.qkvT[:, 0:2, :], B.qkvT[:, 0:2, :], B.root[:, 0:2, :], ALU.mult).then_inc(sem["qk_ready"], 1)
                dve.wait_ge(sem["qk_ready"], n)
                nc.vector.tensor_tensor(B.qke[:], B.qkvT[:, 0:2, :], B.eG[:].unsqueeze(1).to_broadcast([P, 2, TW]), ALU.mult
                                        ).then_inc(sem["grown"], 1)
                dve.wait_ge(sem["k_turned"], n)
                dve.wait_ge(sem["tails_exp"], n)
                dve.wait_ge(sem["act_order"], n)
                nc.vector.tensor_tensor(B.kN[:], tiles(R1), B.tails[:, 0:NT].unsqueeze(2).to_broadcast([P, NT, HD]), ALU.mult
                                        ).then_inc(sem["kN_ready"], 1)
                dve.wait_ge(sem["qk_done"], n)
                dve.wait_ge(sem["masked_decayT"], n)
                nc.vector.tensor_tensor(wide(B.ET), R2[:, 0:TW], wide(B.ET), ALU.mult).then_inc(sem["PT_ready"], 1)
                dve.wait_ge(sem["kk_done"], n)
                dve.wait_ge(sem["masked_decay"], n)
                nc.vector.tensor_tensor(wide(B.A), R1[:, 0:TW], wide(B.EN), ALU.mult).then_inc(sem["A_ready"], 1)
                dve.wait_ge(sem["A_ready"], n)
                level = cst("levels", 0, P).unsqueeze(1).to_broadcast([P, NT, P])
                order.link(nc.vector.tensor_tensor(B.X[:], B.A[:], level, ALU.mult))
                nc.vector.tensor_tensor(B.X[:], cst("ident").unsqueeze(1).to_broadcast([P, NT, P]), B.X[:], ALU.subtract
                                        ).then_inc(sem["X_ready"], 1)
                for l in range(1, LV + 1):
                    dve.wait_ge(sem["YT_done"], h * LV + l)
                    if l < LV:
                        nc.vector.tensor_tensor(wide(B.XT), wide(B.XT), R1[:, 0:TW], ALU.subtract).then_inc(sem["XT_ready"], 1)
                        dve.wait_ge(sem["Y_done"], h * (LV - 1) + l)
                        nc.vector.tensor_tensor(wide(B.X), wide(B.X), R2[:, 0:TW], ALU.subtract).then_inc(sem["X_ready"], 1)
                        dve.wait_ge(sem["XT_ready"], h * (LV + 1) + l + 1)
                        dve.wait_ge(sem["X_ready"], h * (LV + 1) + l + 1)
                    else:
                        order.link(nc.vector.tensor_tensor(wide(B.XT), wide(B.XT), R1[:, 0:TW], ALU.subtract))
                        nc.vector.tensor_tensor(B.XT[:], B.XT[:], cols(B.bcol), ALU.mult).then_inc(sem["XT_ready"], 1)
                dve.sem_inc(sem["X_ready"], 1)
                dve.wait_ge(sem["v_copied"], n)
                dve.wait_ge(sem["ks_done"], h * NT + 1)
                nc.vector.tensor_tensor(B.vN[0:NS, MX, :], B.vN[0:NS, MX, :], R1[0:NS, 0:HD], ALU.subtract
                                        ).then_inc(sem["w_ready"], 1)
                dve.wait_ge(sem["u_copied"], h * NT + 1)
                nc.vector.tensor_scalar(B.um[:], B.uN[:, MX, :], cst("members", NB, NB + 1), None, ALU.mult
                                        ).then_inc(sem["um_ready"], 1)
                dve.wait_ge(sem["ds_done"], h * NT + 1)
                nc.vector.tensor_copy(B.S[:, 0, :], R1[:, 768:896]).then_inc(sem["S_ready"], 1)
                for t in range(PT):
                    c = slice(t * P, (t + 1) * P)
                    dve.wait_ge(sem["ks_done"], h * NT + t + 2)
                    nc.vector.tensor_tensor(B.vN[:, t, :], B.vN[:, t, :], R1[:, c], ALU.subtract).then_inc(sem["w_ready"], 1)
                    dve.wait_ge(sem["ds_done"], h * NT + t + 2)
                    dve.wait_ge(sem["S_ready"], h * NT + t + 1)
                    nc.vector.scalar_tensor_tensor(B.S[:, (t + 1) % 2, :], B.S[:, t % 2, :], B.tails[:, 8 + NB + t:9 + NB + t],
                                                   R1[:, 768:896], ALU.mult, ALU.add
                                                   ).then_inc(sem["S_ready"], 1)
                dve.wait_ge(sem["o_squared"], n)
                nc.vector.tensor_reduce(B.oms[:], B.sqo[:], AX_X, ALU.add).then_inc(sem["o_sums"], 1)
                dve.wait_ge(sem["dss_done"], n)
                dve.wait_ge(sem["scaled_state"], n)
                nc.vector.tensor_tensor(B.sout[:].rearrange("p b v -> p (b v)"), B.sout[:].rearrange("p b v -> p (b v)"), R1[:],
                                        ALU.add).then_inc(sem["state_out_ready"], 1)
                dve.wait_ge(sem["o_root"], n)
                order.link(nc.vector.reciprocal(B.ors[:], B.ort[:]))
                nc.vector.tensor_tensor(B.oN[:], tiles(R2), cols(B.ors, HD), ALU.mult).then_inc(sem["oN_ready"], 1)
                dve.wait_ge(sem["oT_done"], n)
                dve.wait_ge(sem["gate_ready"], n + 1)
                dve.wait_ge(sem["masked_decayT"], n)
                nc.vector.scalar_tensor_tensor(mixT[:, ds(h, 1), :].squeeze(1), R2[:, 0:NY], vecs[:, V_GO:V_GO + 1], B.gz[:],
                                               ALU.mult, ALU.mult).then_inc(sem["turn_done"], 1)
                order.close()

            with dve.Fori(0, HEADS) as h:
                attend(h)

        @block.gpsimd
        def _(pool):
            pool.sem_inc(sem["stores_done"], 1)

            def attend(h):
                n = h + 1
                order = Counter(pool, sem["pool_order"], h, 4)
                pool.wait_ge(sem["turn_done"], n)
                pool.wait_ge(sem["decayT_exp"], n)
                nc.gpsimd.tensor_tensor(wide(B.ET), wide(B.ET), cst("upto"), ALU.mult).then_inc(sem["masked_decayT"], 1)
                pool.wait_ge(sem["decay_exp"], n)
                order.link(nc.gpsimd.tensor_tensor(wide(B.EN), wide(B.EN), cst("after"), ALU.mult))
                pool.wait_ge(sem["gU_ready"], n)
                nc.gpsimd.tensor_tensor(B.EN[:], B.EN[:], cols(B.bcol), ALU.mult).then_inc(sem["masked_decay"], 1)
                pool.wait_ge(sem["state_in"], n * 16)
                pool.wait_ge(sem["tails_exp"], n)
                nc.gpsimd.tensor_tensor(B.sout[:], B.state[:], B.tails[:, 8:8 + NB].unsqueeze(2).to_broadcast([P, NB, HD]),
                                        ALU.mult).then_inc(sem["scaled_state"], 1)
                pool.wait_ge(sem["rows_ready"], n)
                alone(pool, sem["pool_passed"])
                cso = outs["conv_sample"][0].rearrange("b i (s c) -> (b i) s c", s=3)
                cpo = outs["conv_prompt"][0, 0].rearrange("i (s c) -> i s c", s=3)
                pool.dma_start(cso[:, :, ds(h * HD, HD)], B.rowN[0:24]).then_inc(sem["cs_out"], 16)
                pool.dma_start(cpo[:, :, ds(h * HD, HD)], B.rowN[24:27]).then_inc(sem["cp_out"], 16)
                pool.wait_ge(sem["grown"], n)
                nc.gpsimd.tensor_tensor(B.apart[:], B.qke[:, :, NP:NP + NS].unsqueeze(2).to_broadcast([P, 2, NB, NS]),
                                        cst("batch_cols").rearrange("p (b c) -> p b c", b=NB).unsqueeze(1)
                                        .to_broadcast([P, 2, NB, NS]), ALU.mult).then_inc(sem["grown_apart"], 1)
                pool.wait_ge(sem["A_ready"], n)
                for l in range(1, LV + 1):
                    if l >= 3:
                        pool.wait_ge(sem["QT_done"], h * LV + l - 2)
                    nc.gpsimd.tensor_tensor(B.M[:, l % 2], B.A[:], cst("levels", l * P, (l + 1) * P).unsqueeze(1)
                                            .to_broadcast([P, NT, P]), ALU.mult).then_inc(sem["M_ready"], 1)
                pool.wait_ge(sem["u_copied"], h * NT + 1)
                nc.gpsimd.tensor_tensor(B.ub[:], B.uN[:, MX, :].unsqueeze(1).to_broadcast([P, NB, HD]),
                                        cst("members", 0, NB).unsqueeze(2).to_broadcast([P, NB, HD]), ALU.mult
                                        ).then_inc(sem["u_apart"], 1)
                pool.wait_ge(sem["S_ready"], n * NT)
                alone(pool, sem["pool_passed"])
                pool.dma_start(outs["gdn_prompt"][0, 0][ds(h, 1)].squeeze(0), B.S[:, 0, :]).then_inc(sem["gp_out"], 16)
                pool.wait_ge(sem["state_out_ready"], n)
                alone(pool, sem["pool_passed"])
                pool.dma_start(outs["gdn_sample"][0].rearrange("b h k v -> h k b v")[ds(h, 1)].squeeze(0), B.sout[:]
                               ).then_inc(sem["gs_out"], 16)
                for o in ("cs_out", "cp_out", "gp_out", "gs_out"):
                    pool.wait_ge(sem[o], n * 16)
                pool.sem_inc(sem["stores_done"], 1)
                order.close()

            with pool.Fori(0, HEADS) as h:
                attend(h)


def fox_heads(nc, ins, outs, mem, scr):
    cst, xnT, vecs, mixT = mem["cst"], mem["xnT"], mem["vecs"], mem["mixT"]
    AHEAD = 2
    KW = NM + NP
    KS = 2 * P + NS
    ctx, sem, buf = phase(
        nc, "fox",
        PROJECT_SEMS + "turn_done cleared dve_order act_order tanh_og squared sums_q sums_k root_q root_k inverted k_normed "
        "q_normed k_turned v_turned k_copied v_copied past_turned pastT_even pastT_odd index_ready k_past v_past "
        "columns_ready c_rows past_scores scores_copied new_scores s_max s_exp sP_turned sP_copied s_out s_outT "
        "s_rows s_normal scores_done maxed exped P_turned P_copied o_done o_copied o_squared o_sums o_root "
        "oN_ready oT_done gate_ready stores_done k_out v_out km_out vm_out ks_out vs_out pe_passed pool_passed "
        "denominators",
        {
            "w": ([P, SEGS, KT, HD],), "qkvT": ([P, 3, TW],), "th": ([P, NY],), "gz": ([P, NY],),
            "sq": ([P, 2, TW],), "root": ([P, 2, TW],), "kN": ([P, NT, HD],), "vN": ([P, NT, HD],), "vM": ([NM, HD],),
            "cq": ([2, TW],), "ck": ([2, TW],), "lcol": ([P, 1],), "lpast": ([P, PAGES],), "lU": ([P, P],),
            "idxf": ([P, PAGES],), "idx": ([P, PAGES], I32), "kc": ([P, PAGES, HD],), "vc": ([P, PAGES, HD],),
            "kcT": ([P, PAGES, HD],), "gains": ([P, 1],), "sT": ([P, 2 * NS],), "sP": ([NS, KS],), "sPT": ([P, 3 * NS],),
            "sO": ([P, NS],), "smax": ([NS, 1],), "sden": ([NS, 1],), "srec": ([NS, 1],),
            "Pb": ([P, 2, KW],), "PT": ([P, 2, TW],), "pmax": ([P, PT],), "den": ([P, PT],), "rec": ([P, PT],),
            "oN": ([P, NT, HD],), "sqo": ([P, NT, HD],), "oms": ([P, NT],), "ort": ([P, NT],), "ors": ([P, NT],),
        },
        {"pj0": [P, 1024], "pj1": [P, 1024], "R1": [P, 1024], "R2": [P, 1024]},
    )
    B = type("Buffers", (), buf)
    pj, R1, R2 = (B.pj0, B.pj1), B.R1, B.R2
    w_in = ins["w_in"][0].rearrange("(k p) c -> p k c", p=P)
    MC = slice(NP + NS, NPK)
    SC = slice(NP, NP + NS)

    def wide(tile):
        return tile[:].rearrange("p t c -> p (t c)")

    with ctx:
        block = ctx.enter_context(nc.Block())

        @block.sync
        def _(sp):
            sp.wait_ge(sem["cleared"], 4)
            with sp.Fori(0, HEADS) as h:
                load_weights(sp, sem, B.w, w_in, (C_FQ, C_FQ + HEADS * HD, C_FQ + 2 * HEADS * HD, C_OG), h)
                sp.wait_ge(sem["turn_done"], h + 1)
                sp.dma_start(B.cq[0:1, :], scr["c"][0][ds(h, 1)]).then_inc(sem["c_rows"], 16)
                sp.dma_start(B.ck[1:2, :], scr["c"][1][ds(h, 1)]).then_inc(sem["c_rows"], 16)

        @block.tensor
        def _(pe):
            for s in range(SEGS):
                pe.sem_inc(sem[f"projected{s}"], 1)

            def attend(h, ahead):
                n = h + 1
                ident, ones = cst("ident"), cst("ones")
                pe.wait_ge(sem["turn_done"], n)
                pe.wait_ge(sem["squared"], n)
                for region, i, name in ((R1, 0, "sums_q"), (R2, 1, "sums_k")):
                    for a, b in ((0, NP), (NP, TW)):
                        last = nc.tensor.matmul(region[:, a:b], ones, B.sq[:, i, a:b], start=True, stop=True)
                    last.then_inc(sem[name], 1)
                project(nc, pe, sem, B.w, pj, xnT, 2, h)
                pe.wait_ge(sem["root_q"], n)
                pe.wait_ge(sem["k_normed"], n)
                for t in range(NT):
                    last = nc.tensor.transpose(R1[:, t * P:(t + 1) * P], B.qkvT[:, 1, t * P:(t + 1) * P], ident)
                last.then_inc(sem["k_turned"], 1)
                project(nc, pe, sem, B.w, pj, xnT, 3, h)
                pe.wait_ge(sem["root_k"], n)
                pe.wait_ge(sem["evacuated0"], h * 2 + 3)
                for t in range(NT):
                    nc.tensor.transpose(R2[:, t * P:(t + 1) * P], B.qkvT[:, 2, t * P:(t + 1) * P], ident)
                nc.tensor.transpose(R2[0:NM, TW:TW + HD], B.qkvT[:, 2, MC], ident).then_inc(sem["v_turned"], 1)
                pe.wait_ge(sem["k_past"], n * 16 * PAGES)
                for i, (region, name) in enumerate(((R1, "k_copied"), (R2, "v_copied"))):
                    pe.wait_ge(sem[name], n)
                    for j in range(8):
                        last = nc.tensor.transpose(region[:, j * P:(j + 1) * P], B.kc[:, 8 * i + j, :], ident)
                    last.then_inc(sem["past_turned"], 1)
                ahead.take(2)
                pe.wait_ge(sem["pastT_even"], n)
                pe.wait_ge(sem["pastT_odd"], n)
                pe.wait_ge(sem["columns_ready"], n)
                pe.wait_ge(sem["q_normed"], n)
                past = B.lpast[:].rearrange("p (b n) -> p b n", n=2)
                later = past[:, :, 1:2].to_broadcast([P, NB, NQ])
                for page in (1, 0):
                    out = R1[:, page * NS:(page + 1) * NS].rearrange("p (b q) -> p b q", b=NB)
                    nc.tensor.matmul(out, cst("after", 0, P), past[:, :, page:page + 1].to_broadcast([P, NB, NQ]),
                                     start=True, stop=False)
                    if page == 0:
                        nc.tensor.matmul(out, ones, later, start=False, stop=False)
                    nc.tensor.matmul(R1[:, page * NS:(page + 1) * NS], ones, B.lU[:, 0:NS], start=False, stop=False)
                    for b in range(NB):
                        last = nc.tensor.matmul(R1[:, page * NS + NQ * b:page * NS + NQ * (b + 1)], B.kcT[:, 2 * b + page, :],
                                                B.qkvT[:, 0, NP + NQ * b:NP + NQ * (b + 1)], start=False, stop=(b == NB - 1))
                last.then_inc(sem["past_scores"], 1)
                new = R2[0:NS, 2 * P:KS]
                nc.tensor.matmul(new, B.qkvT[:, 0, SC], B.qkvT[:, 1, SC], start=True, stop=False)
                nc.tensor.matmul(new, B.lU[:, 0:NS], cst("after", MX * P, MX * P + NS), start=False, stop=False)
                nc.tensor.matmul(new, ident[:, 0:NS], cst("causal0"), start=False, stop=True)
                ahead.take(2)
                pe.wait_ge(sem["scores_copied"], n)
                for page in range(2):
                    last = nc.tensor.transpose(R2[0:NS, page * P:(page + 1) * P], B.sT[:, page * NS:(page + 1) * NS], ident)
                last.then_inc(sem["new_scores"], 1)
                ahead.take(3)
                pe.wait_ge(sem["s_exp"], n)
                alone(pe, sem["pe_passed"])
                for page in range(2):
                    nc.tensor.transpose(R1[:, page * NS:(page + 1) * NS], B.sP[:, page * P:(page + 1) * P], ident[0:NS, 0:NS])
                nc.tensor.transpose(R1[0:NS, 2 * NS:3 * NS], B.sP[:, 2 * P:], ident[0:NS, 0:NS]).then_inc(sem["sP_turned"], 1)
                ahead.take(2)
                pe.wait_ge(sem["sP_copied"], n)
                pe.wait_ge(sem["v_past"], n * 16 * PAGES)
                nc.tensor.matmul(R1[:, 512:512 + NS], B.vN[0:NS, MX, :], B.sPT[0:NS, 2 * NS:], start=True, stop=False)
                for b in range(NB):
                    for page in range(2):
                        last = nc.tensor.matmul(R1[:, 512 + NQ * b:512 + NQ * (b + 1)], B.vc[:, 2 * b + page, :],
                                                B.sPT[:, page * NS + NQ * b:page * NS + NQ * (b + 1)],
                                                start=False, stop=(b == NB - 1 and page == 1))
                last.then_inc(sem["s_out"], 1)
                ahead.take(2)
                pe.wait_ge(sem["s_outT"], n)
                nc.tensor.transpose(R2[0:NS, 512:640], B.sO[:], ident).then_inc(sem["s_rows"], 1)
                pe.wait_ge(sem["c_rows"], n * 32)

                def scores(i):
                    t, R = i - 1, (R2, R1)[i % 2]
                    q = slice(t * P, (t + 1) * P)
                    if i == 2:
                        pe.wait_ge(sem["s_normal"], n)
                    if i > 2:
                        pe.wait_ge(sem["o_copied"], h * PT + i - 2)
                    width = NM + i * P
                    parts = [(0, NM, NP + NS), (NM, min(width, 512), 0)] + ([(512, width, 512 - NM)] if width > 512 else [])
                    diag = NM + t * P
                    for a, b, key in parts:
                        masked = max(a, diag) < b
                        nc.tensor.matmul(R[:, a:b], B.qkvT[:, 0, q], B.qkvT[:, 1, key:key + b - a], start=True, stop=False)
                        last = nc.tensor.matmul(R[:, a:b], B.cq[:, q], B.ck[:, key:key + b - a], start=False, stop=not masked)
                        if masked:
                            m = max(a, diag)
                            last = nc.tensor.matmul(R[:, m:b], ident, cst("causal", m - diag, b - diag), start=False, stop=True)
                    last.then_inc(sem["scores_done"], 1)

                def outputs(i):
                    R, pb = (R2, R1)[i % 2], i % 2
                    ahead.take(2)
                    pe.wait_ge(sem["exped"], h * PT + i)
                    for j in range(i):
                        nc.tensor.transpose(R[:, j * P:(j + 1) * P], B.Pb[:, pb, NM + j * P:NM + (j + 1) * P], ident)
                    nc.tensor.transpose(R[0:NM, 512:640], B.Pb[:, pb, 0:NM], ident).then_inc(sem["P_turned"], 1)
                    ahead.take(1)
                    pe.wait_ge(sem["P_copied"], h * PT + i)
                    out = R[:, 640:768]
                    nc.tensor.matmul(out, B.PT[0:NM, pb, NP:TW], B.vM[:], start=True, stop=False)
                    for j in range(i):
                        last = nc.tensor.matmul(out, B.PT[:, pb, j * P:(j + 1) * P], B.vN[:, j, :], start=False, stop=(j == i - 1))
                    last.then_inc(sem["o_done"], 1)

                scores(1)
                scores(2)
                for i in range(1, PT + 1):
                    outputs(i)
                    if i + 2 <= PT:
                        scores(i + 2)
                ahead.take(4)
                pe.wait_ge(sem["oN_ready"], n)
                for t in range(NT):
                    a, b = y_cols(t)
                    last = nc.tensor.transpose(R2[:, a:b], B.oN[0:b - a, t, :], ident[0:b - a, 0:b - a])
                last.then_inc(sem["oT_done"], 1)

            def head(h, ahead):
                attend(h, ahead)
                ahead.finish()

            for s in range(AHEAD):
                project(nc, pe, sem, B.w, pj, xnT, s, 0)
            with pe.Fori(0, HEADS - 1) as h:
                head(h, Ahead(h + 1, AHEAD, nc, pe, sem, B.w, pj, xnT))
            head(HEADS - 1, Ahead(None, AHEAD))

        @block.scalar
        def _(act):
            for r in range(2):
                act.sem_inc(sem[f"evacuated{r}"], 1)

            def attend(h):
                n = h + 1
                act.wait_ge(sem["turn_done"], n)
                for s in range(2):
                    act.wait_ge(sem[f"projected{s}"], n + 1)
                    nc.scalar.copy(B.qkvT[:, s, 0:NPK], pj[s % 2][:, 0:NPK]).then_inc(sem[f"evacuated{s % 2}"], 1)
                act.wait_ge(sem["evacuated0"], h * 2 + 2)
                act.wait_ge(sem["evacuated1"], h * 2 + 2)
                nc.scalar.activation(B.sq[:], B.qkvT[:, 0:2, :], ACT.Square).then_inc(sem["squared"], 1)
                for region, i, w in ((R1, 0, "q"), (R2, 1, "k")):
                    act.wait_ge(sem[f"sums_{w}"], n)
                    nc.scalar.activation(B.root[:, i, :], region[:, 0:TW], ACT.Ln, scale=1.0 / HD, bias=cst("eps")
                                         ).then_inc(sem[f"root_{w}"], 1)
                for i, w in ((1, "k"), (0, "q")):
                    act.wait_ge(sem[f"root_{w}"], n)
                    nc.scalar.activation(B.root[:, i, :], B.root[:, i, :], ACT.Exp, scale=-0.5).then_inc(sem["inverted"], 1)
                act.wait_ge(sem["projected2"], n + 1)
                nc.scalar.copy(B.qkvT[:, 2, 0:NPK], pj[0][:, 0:NPK]).then_inc(sem["evacuated0"], 1)
                act.wait_ge(sem["stores_done"], n)
                act.wait_ge(sem["k_turned"], n)
                nc.scalar.copy(wide(B.kN), R1[:, 0:TW]).then_inc(sem["k_copied"], 1)
                act.wait_ge(sem["projected3"], n + 1)
                nc.scalar.activation(B.th[:], pj[1][:, 0:NY], ACT.Tanh, scale=0.5).then_inc(sem["evacuated1"], 1)
                act.wait_ge(sem["v_turned"], n)
                nc.scalar.copy(B.vM[:], R2[0:NM, TW:TW + HD]).then_inc(sem["act_order"], 1)
                nc.scalar.copy(wide(B.vN), R2[:, 0:TW]).then_inc(sem["v_copied"], 1)
                act.wait_ge(sem["past_turned"], h * 2 + 1)
                nc.scalar.copy(B.kcT[:, 0:8, :].rearrange("p n c -> p (n c)"), R1[:]).then_inc(sem["pastT_even"], 1)
                act.wait_ge(sem["s_max"], n)
                nc.scalar.activation(B.sP[:], R2[0:NS, 0:KS], ACT.Exp, bias=B.smax[:], accum_out=B.sden[:]).then_inc(sem["s_exp"], 1)
                act.wait_ge(sem["s_out"], n)
                nc.scalar.copy(B.sO[:], R1[:, 512:512 + NS]).then_inc(sem["s_outT"], 1)
                for i in range(1, PT + 1):
                    t, R, pb = i - 1, (R2, R1)[i % 2], i % 2
                    if i >= 3:
                        act.wait_ge(sem["P_turned"], h * PT + i - 2)
                    act.wait_ge(sem["maxed"], h * PT + i)
                    nc.scalar.activation(B.Pb[:, pb, 0:NM + i * P], R[:, 0:NM + i * P], ACT.Exp, bias=B.pmax[:, t:t + 1],
                                         accum_out=B.den[:, t:t + 1]).then_inc(sem["exped"], 1)
                    act.wait_ge(sem["P_turned"], h * PT + i)
                    nc.scalar.copy(B.PT[0:NM, pb, NP:TW], R[0:NM, 512:640])
                    nc.scalar.copy(B.PT[:, pb, 0:i * P], R[:, 0:i * P]).then_inc(sem["P_copied"], 1)
                act.wait_ge(sem["o_copied"], n * PT)
                act.wait_ge(sem["s_normal"], n)
                nc.scalar.activation(wide(B.sqo), wide(B.oN), ACT.Square).then_inc(sem["o_squared"], 1)
                act.wait_ge(sem["o_sums"], n)
                nc.scalar.activation(B.ort[:], B.oms[:], ACT.Sqrt, scale=1.0 / HD, bias=cst("eps")).then_inc(sem["o_root"], 1)

            with act.Fori(0, HEADS) as h:
                attend(h)

        @block.vector
        def _(dve):
            nc.vector.memset(B.qkvT[:], 0.0).then_inc(sem["cleared"], 1)
            nc.vector.memset(B.oN[:], 0.0).then_inc(sem["cleared"], 1)
            nc.vector.memset(B.cq[:], 1.0).then_inc(sem["cleared"], 1)
            nc.vector.memset(B.ck[:], 1.0).then_inc(sem["cleared"], 1)
            dve.wait_ge(sem["cleared"], 4)
            first = Counter(dve, sem["dve_order"], 0, 20)
            first.link(nc.vector.tensor_scalar(B.gains[:], vecs[:, V_FQ:V_FQ + 1], SCALE, None, ALU.mult))
            first.link(nc.vector.tensor_copy(B.idxf[:], mem["page_rows"][:]))
            first.close()
            dve.sem_inc(sem["turn_done"], 1)

            def attend(h):
                n = h + 1
                order = Counter(dve, sem["dve_order"], n, 20)
                order.link(nc.vector.tensor_copy(B.idx[:], B.idxf[:]))
                nc.vector.tensor_scalar(B.idxf[:], B.idxf[:], 1.0, None, ALU.add).then_inc(sem["index_ready"], 1)
                order.mark(nc.vector.tensor_copy(B.lcol[:], mem["logf_all"][:, MX, ds(h, 1)]))
                order.mark(nc.vector.tensor_copy(B.lpast[:], mem["logf_past"][:, :, ds(h, 1)].rearrange("p n o -> p (n o)")))
                order.wait()
                nc.vector.tensor_scalar(B.lU[:], cst("upto", MX * P), B.lcol[:], None, ALU.mult).then_inc(sem["columns_ready"], 1)
                for i, w, gain in ((1, "k", vecs[:, V_FK:V_FK + 1]), (0, "q", B.gains[:])):
                    dve.wait_ge(sem["inverted"], h * 2 + 2 - i)
                    nc.vector.scalar_tensor_tensor(B.qkvT[:, i, :], B.qkvT[:, i, :], gain, B.root[:, i, :], ALU.mult, ALU.mult
                                                   ).then_inc(sem[f"{w}_normed"], 1)
                dve.wait_ge(sem["evacuated1"], h * 2 + 3)
                nc.vector.tensor_scalar(B.gz[:], B.th[:], 0.5, 0.5, ALU.mult, ALU.add).then_inc(sem["gate_ready"], 1)
                dve.wait_ge(sem["past_turned"], h * 2 + 2)
                nc.vector.tensor_copy(B.kcT[:, 8:16, :].rearrange("p n c -> p (n c)"), R2[:]).then_inc(sem["pastT_odd"], 1)
                dve.wait_ge(sem["past_scores"], n)
                nc.vector.tensor_copy(B.sT[:], R1[:, 0:2 * NS]).then_inc(sem["scores_copied"], 1)
                dve.wait_ge(sem["new_scores"], n)
                nc.vector.tensor_reduce(B.smax[:], R2[0:NS, 0:KS], AX_X, ALU.max, negate=True).then_inc(sem["s_max"], 1)
                dve.wait_ge(sem["sP_turned"], n)
                order.mark(nc.vector.tensor_copy(B.sPT[:, 0:2 * NS], R1[:, 0:2 * NS]))
                nc.vector.tensor_copy(B.sPT[0:NS, 2 * NS:], R1[0:NS, 2 * NS:3 * NS]).then_inc(sem["sP_copied"], 1)
                dve.wait_ge(sem["s_exp"], n)
                order.link(nc.vector.reciprocal(B.srec[:], B.sden[:]))
                dve.wait_ge(sem["s_rows"], n)
                nc.vector.tensor_scalar(B.oN[0:NS, MX, :], R2[0:NS, 512:640], B.srec[:], None, ALU.mult).then_inc(sem["s_normal"], 1)

                def maximum(i):
                    dve.wait_ge(sem["scores_done"], h * PT + i)
                    nc.vector.tensor_reduce(B.pmax[:, i - 1:i], (R2, R1)[i % 2][:, 0:NM + i * P], AX_X, ALU.max, negate=True
                                            ).then_inc(sem["maxed"], 1)

                maximum(1)
                maximum(2)
                for i in range(1, PT + 1):
                    t = i - 1
                    dve.wait_ge(sem["exped"], h * PT + i)
                    order.link(nc.vector.reciprocal(B.rec[:, t:t + 1], B.den[:, t:t + 1]))
                    dve.wait_ge(sem["o_done"], h * PT + i)
                    nc.vector.tensor_scalar(B.oN[:, t, :], (R2, R1)[i % 2][:, 640:768], B.rec[:, t:t + 1], None, ALU.mult
                                            ).then_inc(sem["o_copied"], 1)
                    if i + 2 <= PT:
                        maximum(i + 2)
                dve.wait_ge(sem["o_squared"], n)
                nc.vector.tensor_reduce(B.oms[:], B.sqo[:], AX_X, ALU.add).then_inc(sem["o_sums"], 1)
                dve.wait_ge(sem["o_root"], n)
                order.link(nc.vector.reciprocal(B.ors[:], B.ort[:]))
                nc.vector.tensor_tensor(B.oN[:], B.oN[:], B.ors[:].unsqueeze(2).to_broadcast([P, NT, HD]), ALU.mult
                                        ).then_inc(sem["oN_ready"], 1)
                dve.wait_ge(sem["oT_done"], n)
                dve.wait_ge(sem["gate_ready"], n)
                nc.vector.scalar_tensor_tensor(mixT[:, ds(h + HEADS, 1), :].squeeze(1), R2[:, 0:NY], vecs[:, V_FO:V_FO + 1],
                                               B.gz[:], ALU.mult, ALU.mult).then_inc(sem["turn_done"], 1)
                order.close()

            with dve.Fori(0, HEADS) as h:
                attend(h)

        @block.gpsimd
        def _(pool):
            pool.sem_inc(sem["stores_done"], 1)
            tables = [(ins[t][0].rearrange("n p h d -> (n p h) d"), b, s)
                      for t, b, s in (("cache_k", B.kc, "k_past"), ("cache_v", B.vc, "v_past"))]
            kp, vp = outs["k_prompt"][0, 0], outs["v_prompt"][0, 0]
            ks, vs = (outs[o][0].rearrange("b q h d -> (b q) h d") for o in ("k_sample", "v_sample"))

            def attend(h):
                n = h + 1
                pool.wait_ge(sem["turn_done"], n)
                pool.wait_ge(sem["index_ready"], n)
                alone(pool, sem["pool_passed"])
                for table, place, s in tables:
                    for i in range(PAGES):
                        pool.indirect_dma_start(place[:, i, :], None, table, bass.IndirectOffsetOnAxis(ap=B.idx[:, i:i + 1], axis=0)
                                                ).then_inc(sem[s], 16)
                pool.wait_ge(sem["k_copied"], n)
                pool.wait_ge(sem["v_copied"], n)
                alone(pool, sem["pool_passed"])
                for out, row, all_rows, own in ((kp, ks, B.kN, "k"), (vp, vs, B.vN, "v")):
                    pool.dma_start(out[NM:].rearrange("(t p) h d -> h p t d", p=P)[ds(h, 1)].squeeze(0), all_rows[:, 0:PT, :]
                                   ).then_inc(sem[f"{own}_out"], 16)
                    pool.dma_start(out[0:NM, ds(h, 1), :].squeeze(1), all_rows[NS:T0, MX, :]).then_inc(sem[f"{own}m_out"], 16)
                    pool.dma_start(row[:, ds(h, 1), :].squeeze(1), all_rows[0:NS, MX, :]).then_inc(sem[f"{own}s_out"], 16)
                for o in ("k_out", "km_out", "ks_out", "v_out", "vm_out", "vs_out"):
                    pool.wait_ge(sem[o], n * 16)
                pool.sem_inc(sem["stores_done"], 1)

            with pool.Fori(0, HEADS) as h:
                attend(h)


def mix_out(nc, ins, mem):
    mixT, hres = mem["mixT"], mem["hres"]
    GW = 512
    ctx, sem, buf = phase(
        nc, "out", "w_in0 w_in1 x_in group_done group_added",
        {"w": ([P, 2, KT, GW],)}, {"acc": [P, NT, GW]},
    )
    with ctx:
        w, acc = buf["w"], buf["acc"]
        w_out = ins["w_out"][0].rearrange("(k p) c -> p k c", p=P)
        pairs = D // GW // 2
        block = ctx.enter_context(nc.Block())

        @block.sync
        def _(sp):
            sp.dma_start(hres[:, 0:PT, :], ins["x_prompt"][0].rearrange("(t p) d -> p t d", p=P)).then_inc(sem["x_in"], 16)
            sp.dma_start(hres[0:NS, MX, :], ins["x_sample"].rearrange("b q d -> (b q) d")).then_inc(sem["x_in"], 16)
            with sp.Fori(0, pairs) as i:
                for s in range(2):
                    sp.wait_ge(sem["group_done"], (i * 2 + s) * NT + 2 * NT)
                    sp.dma_start(w[:, s], w_out[:, :, ds((i * 2 + s) * GW, GW)]).then_inc(sem[f"w_in{s}"], 16)

        @block.tensor
        def _(pe):
            pe.sem_inc(sem["group_done"], 2 * NT)
            with pe.Fori(0, pairs) as i:
                for s in range(2):
                    pe.wait_ge(sem[f"w_in{s}"], (i + 1) * 16)
                    for t in range(NT):
                        a, b = y_cols(t)
                        pe.wait_ge(sem["group_added"], (i * 2 + s) * NT + t + 1)
                        for k in range(KT):
                            last = nc.tensor.matmul(acc[0:b - a, t, :], mixT[:, k, a:b], w[:, s, k, :],
                                                    start=(k == 0), stop=(k == KT - 1))
                        last.then_inc(sem["group_done"], 1)

        @block.vector
        def _(dve):
            dve.sem_inc(sem["group_added"], NT)
            dve.wait_ge(sem["x_in"], 32)
            with dve.Fori(0, pairs) as i:
                for s in range(2):
                    for t in range(NT):
                        r = NS if t == MX else P
                        dve.wait_ge(sem["group_done"], (i * 2 + s) * NT + 2 * NT + t + 1)
                        c = ds((i * 2 + s) * GW, GW)
                        nc.vector.tensor_tensor(hres[0:r, t, c], hres[0:r, t, c], acc[0:r, t, :], ALU.add
                                                ).then_inc(sem["group_added"], 1)


def ffn_norm(nc, ins, mem, scr):
    cst, hres, xiT, skT = mem["cst"], mem["hres"], mem["xiT"], mem["skT"]
    ctx, sem, buf = phase(
        nc, "ffn",
        "gain_in keys_in squared rooted reciprocals normed turned copied h_out xi_out0 xi_out1 keys_turned keys_copied",
        {"gain": ([P, D],), "xi": ([P, 2, D],), "sq": ([P, D],), "ss": ([P, NT],), "rt": ([P, NT],), "rs": ([P, NT],),
         "keys": ([P, 2, P],)},
        {"turn": [P, 4, 512], "kps": [P, 2, P]},
    )
    B = type("Buffers", (), buf)
    with ctx:
        block = ctx.enter_context(nc.Block())

        @block.sync
        def _(sp):
            sp.dma_start(B.gain[:], ins["norm_ffn"][0].partition_broadcast(P)).then_inc(sem["gain_in"], 16)
            sp.dma_start(B.keys[:], ins["peer_sub_keys"][0].rearrange("s n c -> n s c")).then_inc(sem["keys_in"], 16)
            sp.dma_start(scr["h"][0:NP].rearrange("(t p) d -> p t d", p=P), hres[:, 0:PT, :]).then_inc(sem["h_out"], 16)
            sp.dma_start(scr["h"][NP:NY], hres[0:NS, MX, :]).then_inc(sem["h_out"], 16)
            for t in range(NT):
                r = NS if t == MX else P
                sp.wait_ge(sem["normed"], t + 1)
                sp.dma_start(scr["xi"][t * P:t * P + r], B.xi[0:r, t % 2, :]).then_inc(sem[f"xi_out{t % 2}"], 16)
            sp.wait_ge(sem["h_out"], 32)
            sp.wait_ge(sem["xi_out0"], 48)
            sp.wait_ge(sem["xi_out1"], 32)

        @block.scalar
        def _(act):
            for t in range(NT):
                r = NS if t == MX else P
                if t >= 1:
                    act.wait_ge(sem["squared"], t)
                nc.scalar.activation(B.sq[0:r, :], hres[0:r, t, :], ACT.Square, accum_out=B.ss[0:r, t:t + 1]
                                     ).then_inc(sem["squared"], 1)
                act.wait_ge(sem["squared"], t + 1)
                nc.scalar.activation(B.rt[0:r, t:t + 1], B.ss[0:r, t:t + 1], ACT.Sqrt, scale=1.0 / D, bias=cst("eps")[0:r]
                                     ).then_inc(sem["rooted"], 1)

        @block.vector
        def _(dve):
            dve.wait_ge(sem["gain_in"], 16)
            for t in range(NT):
                r = NS if t == MX else P
                dve.wait_ge(sem["rooted"], t + 1)
                nc.vector.reciprocal(B.rs[0:r, t:t + 1], B.rt[0:r, t:t + 1]).then_inc(sem["reciprocals"], 1)
                dve.wait_ge(sem["reciprocals"], t + 1)
                if t >= 2:
                    dve.wait_ge(sem["turned"], 4 * (t - 1))
                    dve.wait_ge(sem[f"xi_out{t % 2}"], 16 * (t // 2))
                nc.vector.scalar_tensor_tensor(B.xi[0:r, t % 2, :], hres[0:r, t, :], B.rs[0:r, t:t + 1], B.gain[0:r, :],
                                               ALU.mult, ALU.mult).then_inc(sem["normed"], 1)
                a, b = y_cols(t)
                for g in range(4):
                    dve.wait_ge(sem["turned"], 4 * t + g + 1)
                    nc.vector.tensor_copy(xiT[:, 4 * g:4 * g + 4, a:b],
                                          B.turn[:, g, :].rearrange("p (k t) -> p k t", k=4)[:, :, 0:r]
                                          ).then_inc(sem["copied"], 1)
            dve.wait_ge(sem["keys_turned"], 1)
            nc.vector.tensor_copy(skT[:], B.kps[:]).then_inc(sem["keys_copied"], 1)

        @block.tensor
        def _(pe):
            for t in range(NT):
                r = NS if t == MX else P
                pe.wait_ge(sem["normed"], t + 1)
                for g in range(4):
                    if t >= 1:
                        pe.wait_ge(sem["copied"], 4 * (t - 1) + g + 1)
                    for k in range(4):
                        last = nc.tensor.transpose(B.turn[:, g, k * P:k * P + r],
                                                   B.xi[0:r, t % 2, (4 * g + k) * P:(4 * g + k + 1) * P],
                                                   cst("ident")[0:r, 0:r])
                    last.then_inc(sem["turned"], 1)
            pe.wait_ge(sem["keys_in"], 16)
            for s in range(2):
                last = nc.tensor.transpose(B.kps[:, s, :], B.keys[:, s, :], cst("ident"))
            last.then_inc(sem["keys_turned"], 1)


def route(nc, ins, mem):
    cst, xiT, skT = mem["cst"], mem["xiT"], mem["skT"]
    ctx, sem, buf = phase(
        nc, "route",
        "w_in0 w_in1 projected0 projected1 query_copied0 query_copied1 scored0 scored1 scores_copied0 scores_copied1 "
        "scores_read cleared dve_passed dve_order centred exped sums_ready act_order",
        {"w": ([P, 2, KT, P],), "q": ([P, 2, NY],), "sc": ([P, NT, 2, KEYS],), "top": ([P, NT, 2, TOPK],),
         "at": ([P, NT, 2, TOPK], U32), "atf": ([P, NT, 2, TOPK],), "cand": ([P, NT, TOPK, TOPK],),
         "best": ([P, NT, TOPK],), "pos": ([P, NT, TOPK], U32), "pos2": ([P, 2, NT, TOPK], U32),
         "posf": ([P, 2, NT, TOPK],), "hot": ([P, NT, TOPK, TOPK],), "pick": ([P, 2, NT, TOPK],),
         "gate": ([P, NT, TOPK],), "sum": ([P, NT],), "rec": ([P, NT],)},
        {"pq0": [P, 1024], "pq1": [P, 1024], "ps0": [P, 1024], "ps1": [P, 1024]},
    )
    B = type("Buffers", (), buf)
    pq, ps = (B.pq0, B.pq1), (B.ps0, B.ps1)
    w_q = ins["peer_w_query"][0].rearrange("(k p) c -> p k c", p=P)
    LOW = -3.0e38
    with ctx:
        block = ctx.enter_context(nc.Block())

        @block.sync
        def _(sp):
            with sp.Fori(0, HEADS) as h:
                for s in range(2):
                    sp.wait_ge(sem[f"projected{s}"], h + 1)
                    sp.dma_start(B.w[:, s], w_q[:, :, ds(h * 2 * P + s * P, P)]).then_inc(sem[f"w_in{s}"], 16)

        @block.tensor
        def _(pe):
            for s in range(2):
                pe.sem_inc(sem[f"projected{s}"], 1)
            with pe.Fori(0, HEADS) as h:
                for s in range(2):
                    pe.wait_ge(sem[f"w_in{s}"], (h + 1) * 16)
                    pe.wait_ge(sem[f"query_copied{s}"], h + 1)
                    for k in range(KT):
                        for a, b in ((0, NP), (NP, NY)):
                            last = nc.tensor.matmul(pq[s][:, a:b], B.w[:, s, k, :], xiT[:, k, a:b], start=(k == 0),
                                                    stop=(k == KT - 1))
                    last.then_inc(sem[f"projected{s}"], 1)
                for s in range(2):
                    pe.wait_ge(sem[f"query_copied{s}"], h + 2)
                    pe.wait_ge(sem[f"scores_copied{s}"], h + 1)
                    for t in range(NT):
                        a, b = y_cols(t)
                        last = nc.tensor.matmul(ps[s][0:b - a, t * KEYS:(t + 1) * KEYS], B.q[:, s, a:b], skT[:, s, :],
                                                start=True, stop=True)
                    last.then_inc(sem[f"scored{s}"], 1)

        @block.scalar
        def _(act):
            for s in range(2):
                act.sem_inc(sem[f"query_copied{s}"], 1)
                act.sem_inc(sem[f"scores_copied{s}"], 1)
            act.wait_ge(sem["cleared"], 2)
            with act.Fori(0, HEADS) as h:
                for s in range(2):
                    act.wait_ge(sem[f"projected{s}"], h + 2)
                    act.wait_ge(sem[f"scored{s}"], h + 1)
                    nc.scalar.copy(B.q[:, s, :], pq[s][:, 0:NY]).then_inc(sem[f"query_copied{s}"], 1)
                for s in range(2):
                    act.wait_ge(sem[f"scored{s}"], h + 2)
                    act.wait_ge(sem["scores_read"], h + 1)
                    nc.scalar.copy(B.sc[0:NS, MX, s, :], ps[s][0:NS, MX * KEYS:NT * KEYS])
                    nc.scalar.copy(B.sc[:, 0:PT, s, :], ps[s][:, 0:PT * KEYS].rearrange("p (t n) -> p t n", t=PT)
                                   ).then_inc(sem[f"scores_copied{s}"], 1)
                act.wait_ge(sem["centred"], h + 1)
                nc.scalar.activation(B.gate[:], B.gate[:], ACT.Exp).then_inc(sem["exped"], 1)

        @block.vector
        def _(dve):
            nc.vector.memset(B.top[:], 0.0).then_inc(sem["cleared"], 1)
            nc.vector.memset(B.at[:], 0).then_inc(sem["cleared"], 1)
            nc.vector.memset(B.best[:], 0.0).then_inc(sem["cleared"], 1)
            nc.vector.memset(B.pos[:], 0).then_inc(sem["cleared"], 1)
            dve.wait_ge(sem["cleared"], 4)
            dve.sem_inc(sem["scores_read"], 1)
            for s in range(2):
                dve.sem_inc(sem[f"scored{s}"], 1)

            def top16(order, items):
                def settle():
                    order.wait()
                    alone(dve, sem["dve_passed"])

                alone(dve, sem["dve_passed"])
                for half in range(2):
                    at = slice(8 * half, 8 * half + 8)
                    for values, best, place in items:
                        order.mark(nc.vector.max(best[..., at], values))
                    settle()
                    for values, best, place in items:
                        order.mark(nc.vector.max_index(place[..., at], best[..., at], values))
                    settle()
                    if half == 0:
                        for values, best, place in items:
                            order.mark(nc.vector.match_replace(values, best[..., at], values, LOW))
                        settle()

            with dve.Fori(0, HEADS) as h:
                order = Counter(dve, sem["dve_order"], h, 100)
                for s in range(2):
                    dve.wait_ge(sem[f"scores_copied{s}"], h + 2)
                rows = [slice(0, NS if t == MX else P) for t in range(NT)]
                top16(order, [(B.sc[rows[t], t, s, :], B.top[rows[t], t, s, :], B.at[rows[t], t, s, :])
                              for t in range(NT) for s in range(2)])
                dve.sem_inc(sem["scores_read"], 1)
                order.mark(nc.vector.tensor_copy(B.atf[:], B.at[:]))
                order.link(nc.vector.tensor_tensor(B.cand[:], B.top[:, :, 0, :].unsqueeze(3).to_broadcast([P, NT, TOPK, TOPK]),
                                                   B.top[:, :, 1, :].unsqueeze(2).to_broadcast([P, NT, TOPK, TOPK]), ALU.add))
                top16(order, [(B.cand[rows[t], t].rearrange("p a b -> p (a b)"), B.best[rows[t], t, :], B.pos[rows[t], t, :])
                              for t in range(NT)])
                nc.vector.tensor_tensor(B.gate[:], B.best[:], B.best[:, :, 0:1].to_broadcast([P, NT, TOPK]), ALU.subtract
                                        ).then_inc(sem["centred"], 1)
                order.mark(nc.vector.tensor_scalar(B.pos2[:, 0], B.pos[:], 4, None, ALU.logical_shift_right))
                order.mark(nc.vector.tensor_scalar(B.pos2[:, 1], B.pos[:], TOPK - 1, None, ALU.bitwise_and))
                order.wait()
                order.link(nc.vector.tensor_copy(B.posf[:], B.pos2[:]))
                for s in range(2):
                    order.link(nc.vector.tensor_tensor(
                        B.hot[:], B.posf[:, s].unsqueeze(3).to_broadcast([P, NT, TOPK, TOPK]),
                        cst("iota").unsqueeze(1).unsqueeze(1).to_broadcast([P, NT, TOPK, TOPK]), ALU.is_equal))
                    order.link(nc.vector.tensor_tensor(
                        B.hot[:], B.hot[:], B.atf[:, :, s, :].unsqueeze(2).to_broadcast([P, NT, TOPK, TOPK]), ALU.mult))
                    order.link(nc.vector.tensor_reduce(B.pick[:, s], B.hot[:], AX_X, ALU.add))
                order.link(nc.vector.scalar_tensor_tensor(B.pick[:, 0], B.pick[:, 0], float(KEYS), B.pick[:, 1],
                                                          ALU.mult, ALU.add))
                order.mark(nc.vector.tensor_copy(mem["idx_all"][:, :, ds(h, 1), :].squeeze(2), B.pick[:, 0]))
                dve.wait_ge(sem["exped"], h + 1)
                order.link(nc.vector.tensor_reduce(B.sum[:], B.gate[:], AX_X, ALU.add))
                order.link(nc.vector.reciprocal(B.rec[:], B.sum[:]))
                order.link(nc.vector.tensor_tensor(mem["gate_all"][:, :, ds(h, 1), :].squeeze(2), B.gate[:],
                                                   B.rec[:].unsqueeze(2).to_broadcast([P, NT, TOPK]), ALU.mult))
                order.close()


def experts(nc, ins, outs, mem, scr):
    cst = mem["cst"]
    RING = 16
    GROUPS = HEADS
    FOLD = P // NS
    SG = HEADS // FOLD
    NG = SG + PT * GROUPS
    names = " ".join(f"landed{m}" for m in range(RING))
    ctx, sem, buf = phase(
        nc, "exp",
        names + " table_ready spread consumed admitted pool_order xi_in h_in hidden activated weighed y_free y_out "
        "sample_in cleared dve_passed folded fold_copied ys_out",
        {"ring": ([P, RING, D],), "xi": ([P, D],), "y": ([P, D],), "idx_x": ([P, NG * TOPK], I32),
         "gate_x": ([P, NG * TOPK],), "idx_c": ([P, 2, 8, 2], I32), "hid": ([P, TOPK],), "act": ([P, TOPK],),
         "wt": ([P, TOPK],), "ys": ([NS, D],)},
        {"fold": [NS, 4, 512]},
    )
    B = type("Buffers", (), buf)
    idx_all, gate_all = mem["idx_all"], mem["gate_all"]

    def items(first, i):
        return first + RING + (i - 1) * 2 * TOPK

    def tile_first(t):
        return SG * 2 * TOPK + t * (GROUPS * 2 * TOPK)

    with ctx:
        block = ctx.enter_context(nc.Block())

        @block.sync
        def _(sp):
            for r in range(FOLD):
                for table, source in ((B.idx_x, idx_all), (B.gate_x, gate_all)):
                    sp.dma_start(table[r * NS:(r + 1) * NS, 0:SG * TOPK],
                                 source[0:NS, MX, r * SG:(r + 1) * SG, :].rearrange("p h k -> p (h k)")).then_inc(sem["spread"], 16)
                sp.dma_start(B.xi[r * NS:(r + 1) * NS, :], scr["xi"][NP:NY]).then_inc(sem["sample_in"], 16)
            sp.wait_ge(sem["cleared"], 1)
            sp.dma_start(B.y[0:NS, :], scr["h"][NP:NY]).then_inc(sem["sample_in"], 16)
            with sp.Fori(0, PT) as t:
                sp.wait_ge(sem["consumed"], t * (GROUPS * 2 * TOPK) + (tile_first(0) - 1))
                sp.dma_start(B.xi[:], scr["xi"][ds(t * P, P)]).then_inc(sem["xi_in"], 16)
                sp.wait_ge(sem["y_free"], t + 1)
                sp.dma_start(B.y[:], scr["h"][ds(t * P, P)]).then_inc(sem["h_in"], 16)
            sp.wait_ge(sem["fold_copied"], 1)
            sp.dma_start(outs["y_sample"].rearrange("b q d -> (b q) d"), B.ys[:]).then_inc(sem["ys_out"], 16)
            sp.wait_ge(sem["ys_out"], 16)

        @block.gpsimd
        def _(pool):
            pool.wait_ge(sem["table_ready"], 2)
            pool.wait_ge(sem["spread"], 32 * FOLD)
            u, v = ins["peer_u"][0], ins["peer_v"][0]

            def gather(table, half, k, which, item, place):
                pool.wait_ge(sem["consumed"], item + 1)
                alone(pool, sem["admitted"])
                pool.indirect_dma_start(B.ring[:, place, :], None, table,
                                        bass.IndirectOffsetOnAxis(ap=B.idx_c[:, half, k, which:which + 1], axis=0)
                                        ).then_inc(sem[f"landed{place}"], 16)

            def half_turn(group, first, half, turns, gap, with_u=True, with_v=True):
                pool.wait_ge(sem["consumed"], first + (RING - gap))
                for which, g in ((0, group if with_u else group - 1), (1, group - 1 if with_v else group)):
                    source = B.idx_x[:, ds(g * TOPK + half * 8, 8)]
                    nc.gpsimd.tensor_copy(B.idx_c[:, half, :, which], source).then_inc(sem["pool_order"], 1)
                pool.wait_ge(sem["pool_order"], (turns + 1) * 2)
                item = 0
                for k in range(8):
                    for which, wanted, table in ((0, with_u, u), (1, with_v, v)):
                        if wanted:
                            place = (item + (8 * half if with_u != with_v else 0)) % RING
                            gather(table, half, k, which, first + item, place)
                            item += 1

            def tile(first, group0, groups, turns):
                for half in range(2):
                    half_turn(group0, first + 8 * half, half, turns + half, 8, with_v=False)

                def middle(i):
                    for half in range(2):
                        half_turn(group0 + i, items(first, i) + TOPK * half, half, turns + i * 2 + half, RING)
                pool.wait_ge(sem["consumed"], first + (RING + 8))
                alone(pool, sem["admitted"])
                if groups == 2:
                    middle(1)
                else:
                    with pool.Fori(1, groups) as i:
                        middle(i)
                for half in range(2):
                    half_turn(group0 + groups, items(first, groups) + 8 * half, half, turns + groups * 2 + half, RING if half == 0 else 8,
                              with_u=False)

            tile(0, 0, SG, 0)
            with pool.Fori(0, PT) as t:
                tile(tile_first(t), t * GROUPS + SG, GROUPS, t * (2 * GROUPS + 2) + (2 * SG + 2))

        @block.scalar
        def _(act):
            def activate(done):
                act.wait_ge(sem["hidden"], done + 1)
                nc.scalar.activation(B.act[:], B.hid[:], ACT.Gelu).then_inc(sem["activated"], 1)

            for g in range(SG):
                activate(g)
            act.wait_ge(sem["folded"], 1)
            nc.scalar.copy(B.ys[:], B.fold[:].rearrange("p a b -> p (a b)")).then_inc(sem["fold_copied"], 1)
            act.sem_inc(sem["y_free"], 1)
            with act.Fori(0, PT) as t:
                with act.Fori(0, GROUPS) as g:
                    activate(t * GROUPS + g + SG)
                act.wait_ge(sem["consumed"], tile_first(t) + (GROUPS * 2 * TOPK + RING))
                act.dma_start(outs["y_prompt"][0][ds(t * P, P)], B.y[:]).then_inc(sem["y_out"], 16)
                act.wait_ge(sem["y_out"], (t + 1) * 16)
                act.sem_inc(sem["y_free"], 1)

        @block.vector
        def _(dve):
            nc.vector.memset(B.y[:], 0.0).then_inc(sem["cleared"], 1)
            for table, source in ((B.idx_x, idx_all), (B.gate_x, gate_all)):
                nc.vector.tensor_copy(table[:, SG * TOPK:].rearrange("p (t h k) -> p t h k", t=PT, h=HEADS),
                                      source[:, 0:PT, :, :]).then_inc(sem["table_ready"], 1)
            dve.wait_ge(sem["table_ready"], 2)
            dve.wait_ge(sem["spread"], 32 * FOLD)
            dve.sem_inc(sem["consumed"], RING)

            def hidden(k, item, place, turn):
                dve.wait_ge(sem[f"landed{place}"], turn * 16 + 16)
                nc.vector.tensor_tensor_reduce(B.ring[:, place, :], B.ring[:, place, :], B.xi[:], 1.0, 0.0, ALU.mult, ALU.add,
                                               B.hid[:, k:k + 1]).then_inc(sem["consumed"], 1)

            def add(k, item, place, turn, behind):
                dve.wait_ge(sem[f"landed{place}"], turn * 16 + 16)
                dve.wait_ge(sem["consumed"], item + (RING + 1 - behind))
                nc.vector.scalar_tensor_tensor(B.y[:], B.ring[:, place, :], B.wt[:, k:k + 1], B.y[:], ALU.mult, ALU.add
                                               ).then_inc(sem["consumed"], 1)

            def weigh(group, after):
                dve.wait_ge(sem["consumed"], after + RING)
                dve.sem_inc(sem["hidden"], 1)
                dve.wait_ge(sem["activated"], group + 1)
                nc.vector.tensor_tensor(B.wt[:], B.act[:], B.gate_x[:, ds(group * TOPK, TOPK)], ALU.mult
                                        ).then_inc(sem["weighed"], 1)
                dve.wait_ge(sem["weighed"], group + 1)

            def tile(first, group0, groups, uses, start):
                for k in range(TOPK):
                    hidden(k, first + k, k, uses)
                weigh(group0, first + TOPK)
                start()
                alone(dve, sem["dve_passed"])

                def middle(i):
                    for m in range(2 * TOPK):
                        turn = uses + i * 2 + (m // RING - 1)
                        if m % 2 == 0:
                            hidden(m // 2, items(first, i) + m, m % RING, turn)
                        else:
                            add(m // 2, items(first, i) + m, m % RING, turn, 2 if m > 1 else 2)
                    weigh(group0 + i, items(first, i) + 2 * TOPK)
                if groups == 2:
                    middle(1)
                else:
                    with dve.Fori(1, groups) as i:
                        middle(i)
                for k in range(TOPK):
                    add(k, items(first, groups) + k, k, uses + 2 * groups - 1, 1)

            dve.wait_ge(sem["sample_in"], 16 * (FOLD + 1))
            tile(0, 0, SG, 0, lambda: None)
            with dve.Fori(0, PT) as t:
                dve.wait_ge(sem["xi_in"], t * 16 + 16)
                tile(tile_first(t), t * GROUPS + SG, GROUPS, t * (2 * GROUPS) + 2 * SG,
                     lambda: dve.wait_ge(sem["h_in"], t * 16 + 16))

        @block.tensor
        def _(pe):
            pe.wait_ge(sem["consumed"], SG * 2 * TOPK + RING)
            for c in range(4):
                last = nc.tensor.matmul(B.fold[:, c, :], cst("fold"), B.y[:, c * 512:(c + 1) * 512], start=True, stop=True)
            last.then_inc(sem["folded"], 1)


_OUTS = {
    "y_prompt": (1, NP, D), "y_sample": (NB, NQ, D),
    "k_prompt": (1, 1, NM + NP, HEADS, HD), "v_prompt": (1, 1, NM + NP, HEADS, HD), "logf_prompt": (1, 1, NM + NP, HEADS),
    "gdn_prompt": (1, 1, HEADS, HD, HD), "conv_prompt": (1, 1, CONV - 1, 3 * HEADS * HD),
    "k_sample": (1, NB, NQ, HEADS, HD), "v_sample": (1, NB, NQ, HEADS, HD), "logf_sample": (1, NB, NQ, HEADS),
    "gdn_sample": (1, NB, HEADS, HD, HD), "conv_sample": (1, NB, CONV - 1, 3 * HEADS * HD),
}


def kernel(**inputs):
    import concourse.bacc as _bacc
    from concourse.bass_utils import run_bass_kernel_spmd as _run

    nc = _bacc.Bacc("TRN2", target_bir_lowering=False, num_devices=1)
    arrays, ins, outs = {}, {}, {}
    for name, a in {**inputs, "constants": constant_array()}.items():
        a = np.ascontiguousarray(a)
        arrays[f"in_{name}_dram"] = a
        ins[name] = nc.dram_tensor(f"in_{name}_dram", a.shape, mybir.dt.from_np(a.dtype), kind="ExternalInput").ap()
    for name, shape in _OUTS.items():
        outs[name] = nc.dram_tensor(f"out_{name}_dram", shape, F32, kind="ExternalOutput").ap()
    build(nc, ins, outs)
    r = _run(nc, [arrays], core_ids=[0])
    return tuple(r.results[0][f"out_{name}_dram"] for name in _OUTS)
```
